# Optimizing a Trainium2 kernel written in Bass

```python
import jax, jax.numpy as jnp
from jax import lax
import numpy as np

D_MODEL = 1024
BATCH = 1
SEQ = 1024
DEPTH = 2

GRID_W = 64
CTX_LEN = 256
N_EVEN = (DEPTH + 1) // 2
N_ODD = DEPTH // 2
MOD_CHUNKS = 6
EPS = 1e-6
CHUNK = 128
GMLP_GROUP_W = 128
D_GMLP = D_MODEL // 2
GMLP_GROUPS = D_GMLP // GMLP_GROUP_W
FOURIER_GROUP_W = 128
D_FOURIER = D_MODEL // 2
FOURIER_GROUPS = D_FOURIER // FOURIER_GROUP_W
EVEN_IN = 2 * D_GMLP + D_FOURIER
EVEN_MIX = D_GMLP + D_FOURIER
HEAD_DIM = 64
N_HEADS = (D_MODEL // 2) // HEAD_DIM
N_KV_HEADS = 2
Q_PER_KV = N_HEADS // N_KV_HEADS
WINDOW = 128
ATT_BLOCK = 128
AXIS_DIM = HEAD_DIM // 2
ROPE_BASE = 10000.0
D_CONV = D_MODEL // 2
CONV_WIDTH = 3
Q_W = N_HEADS * HEAD_DIM
KV_W = N_KV_HEADS * HEAD_DIM
ODD_SPLITS = (Q_W, Q_W + KV_W, Q_W + 2 * KV_W, Q_W + 2 * KV_W + D_CONV, Q_W + 2 * KV_W + 2 * D_CONV)
ODD_IN = Q_W + 2 * KV_W + 3 * D_CONV
ODD_MIX = Q_W + D_CONV
N_EXPERTS = 64
TOP_K = 6
D_EXPERT = 256
D_SHARED = 256
ROUTED_SCALE = 2.5
EXPERT_BLOCK = 128

kernel_name = "hybrid_gmlp_fourier_swa_conv_moe_dit"

def rms_norm(x, g):
    xf = x.astype(jnp.float32)
    y = xf * lax.rsqrt(jnp.mean(xf * xf, axis=-1, keepdims=True) + EPS)
    return (y * g.astype(jnp.float32)).astype(x.dtype)

def modulation(cond, w, b):
    m = jax.nn.silu(cond) @ w + b
    return jnp.split(m[..., None, :], MOD_CHUNKS, axis=-1)

def modulate(h, shift, scale):
    return h * (1 + scale) + shift

def axial_rope_tables(n_tok):
    rows = n_tok // GRID_W
    r = jnp.repeat(jnp.arange(rows, dtype=jnp.float32), GRID_W)
    col = jnp.tile(jnp.arange(GRID_W, dtype=jnp.float32), rows)
    inv = ROPE_BASE ** (-jnp.arange(0, AXIS_DIM, 2, dtype=jnp.float32) / AXIS_DIM)
    ang = jnp.stack([r[:, None] * inv, col[:, None] * inv], axis=1)
    return jnp.cos(ang), jnp.sin(ang)

def apply_axial_rope(x, cos, sin):
    b, s, h, _ = x.shape
    xr = x.reshape(b, s, h, 2, 2, AXIS_DIM // 2)
    x1, x2 = xr[..., 0, :], xr[..., 1, :]
    cs = cos[:, None].astype(x.dtype)
    sn = sin[:, None].astype(x.dtype)
    out = jnp.stack([x1 * cs - x2 * sn, x2 * cs + x1 * sn], axis=-2)
    return out.reshape(x.shape)

def heads(t, n):
    return t.reshape(t.shape[0], t.shape[1], n, HEAD_DIM)

def gmlp_spatial_gating(u, v, w_s, b_s):
    b, L, _ = u.shape
    nc = L // CHUNK
    u = jax.nn.gelu(u).reshape(b, nc, CHUNK, GMLP_GROUPS, GMLP_GROUP_W)
    vf = jax.nn.gelu(v).astype(jnp.float32).reshape(b, nc, CHUNK, GMLP_GROUPS, GMLP_GROUP_W)
    mu = jnp.mean(vf, axis=-1, keepdims=True)
    var = jnp.mean(jnp.square(vf - mu), axis=-1, keepdims=True)
    vn = ((vf - mu) * lax.rsqrt(var + 1e-5)).astype(u.dtype)
    f = jnp.einsum("gpq,bnqgc->bnpgc", w_s, vn) + b_s.T[:, :, None]
    return (u * f).reshape(b, L, D_GMLP)

def fourier_mix(f):
    b, L, _ = f.shape
    fg = f.astype(jnp.float32).reshape(b, L, FOURIER_GROUPS, FOURIER_GROUP_W)
    y = jnp.fft.fft2(fg, axes=(1, 3), norm="ortho").real
    return y.astype(f.dtype).reshape(b, L, D_FOURIER)

def even_mixer(h, w_in, w_s, b_s, w_out):
    u, v, f = jnp.split(h @ w_in, [D_GMLP, 2 * D_GMLP], axis=-1)
    mixed = jnp.concatenate([gmlp_spatial_gating(u, v, w_s, b_s), fourier_mix(f)], axis=-1)
    return mixed @ w_out

def short_conv(g_in, g_out, z_in, w):
    z = g_in * z_in
    L = z.shape[1]
    pad = CONV_WIDTH // 2
    zp = jnp.pad(z, ((0, 0), (pad, pad), (0, 0)))
    y = zp[:, 0:L] * w[0]
    for j in range(1, CONV_WIDTH):
        y = y + zp[:, j:j + L] * w[j]
    return g_out * y

def sink_softmax(parts, sink):
    m = sink
    for s in parts:
        m = jnp.maximum(m, jnp.max(s, axis=-1, keepdims=True))
    den = jnp.exp(sink - m)
    es = []
    for s in parts:
        e = jnp.exp(s - m)
        den = den + jnp.sum(e, axis=-1, keepdims=True)
        es.append(e)
    return [e / den for e in es]

def latent_window_attention(q, k, v, kc, vc, sink):
    b, s, _, dh = q.shape
    nb = s // ATT_BLOCK
    scale = dh ** -0.5
    qb = q.reshape(b, nb, ATT_BLOCK, N_KV_HEADS, Q_PER_KV, dh)

    def band(t):
        tb = t.reshape(b, nb, ATT_BLOCK, N_KV_HEADS, dh)
        tp = jnp.pad(tb, ((0, 0), (1, 1), (0, 0), (0, 0), (0, 0)))
        return jnp.concatenate([tp[:, :-2], tp[:, 1:-1], tp[:, 2:]], axis=2)

    kb, vb = band(k), band(v)
    s_band = jnp.einsum("bnqhgd,bnkhd->bnhgqk", qb, kb).astype(jnp.float32) * scale
    blk = jnp.arange(nb)[:, None, None]
    qpos = blk * ATT_BLOCK + jnp.arange(ATT_BLOCK)[None, :, None]
    kpos = (blk - 1) * ATT_BLOCK + jnp.arange(3 * ATT_BLOCK)[None, None, :]
    valid = (jnp.abs(kpos - qpos) <= WINDOW) & (kpos >= 0) & (kpos < s)
    s_band = jnp.where(valid[None, :, None, None], s_band, -jnp.inf)
    s_ctx = jnp.einsum("bnqhgd,bkhd->bnhgqk", qb, kc).astype(jnp.float32) * scale
    snk = sink.astype(jnp.float32).reshape(1, 1, N_KV_HEADS, Q_PER_KV, 1, 1)
    p_band, p_ctx = sink_softmax([s_band, s_ctx], snk)
    o = (jnp.einsum("bnhgqk,bnkhd->bnqhgd", p_band.astype(v.dtype), vb)
         + jnp.einsum("bnhgqk,bkhd->bnqhgd", p_ctx.astype(v.dtype), vc))
    return o.reshape(b, s, N_HEADS * dh)

def context_attention(qc, kc, vc, sink):
    b, lc, _, dh = qc.shape
    qg = qc.reshape(b, lc, N_KV_HEADS, Q_PER_KV, dh)
    sc = jnp.einsum("bqhgd,bkhd->bhgqk", qg, kc).astype(jnp.float32) * dh ** -0.5
    snk = sink.astype(jnp.float32).reshape(1, N_KV_HEADS, Q_PER_KV, 1, 1)
    (p,) = sink_softmax([sc], snk)
    o = jnp.einsum("bhgqk,bkhd->bqhgd", p.astype(vc.dtype), vc)
    return o.reshape(b, lc, N_HEADS * dh)

def odd_mixer(h, hc, w_in, q_g, k_g, sink, conv_w, w_out, cos, sin, ctx_out):
    q, k, v, g_in, g_out, z = jnp.split(h @ w_in, list(ODD_SPLITS), axis=-1)
    q = apply_axial_rope(rms_norm(heads(q, N_HEADS), q_g), cos, sin)
    k = apply_axial_rope(rms_norm(heads(k, N_KV_HEADS), k_g), cos, sin)
    v = heads(v, N_KV_HEADS)
    if ctx_out:
        qc, kc, vc, gc_in, gc_out, zc = jnp.split(hc @ w_in, list(ODD_SPLITS), axis=-1)
    else:
        kc, vc = jnp.split(hc @ w_in[:, Q_W:Q_W + 2 * KV_W], 2, axis=-1)
    kc = rms_norm(heads(kc, N_KV_HEADS), k_g)
    vc = heads(vc, N_KV_HEADS)
    y = jnp.concatenate([latent_window_attention(q, k, v, kc, vc, sink),
                         short_conv(g_in, g_out, z, conv_w)], axis=-1) @ w_out
    if not ctx_out:
        return y, None
    qc = rms_norm(heads(qc, N_HEADS), q_g)
    yc = jnp.concatenate([context_attention(qc, kc, vc, sink),
                          short_conv(gc_in, gc_out, zc, conv_w)], axis=-1) @ w_out
    return y, yc

def swiglu(x, w1, w3, w2):
    return (jax.nn.silu(x @ w1) * (x @ w3)) @ w2

def routed_experts(xf, idx, gates, w1, w3, w2):
    n, d = xf.shape
    nk = n * TOP_K
    flat_e = idx.reshape(-1)
    flat_g = gates.reshape(-1)
    flat_tok = jnp.arange(nk, dtype=jnp.int32) // TOP_K
    order = jnp.argsort(flat_e)
    sorted_e = flat_e[order]
    counts = jax.ops.segment_sum(jnp.ones((nk,), jnp.int32), flat_e, num_segments=N_EXPERTS)
    padded = (counts + EXPERT_BLOCK - 1) // EXPERT_BLOCK * EXPERT_BLOCK
    pend = jnp.cumsum(padded)
    pstart = pend - padded
    start = jnp.cumsum(counts) - counts
    dest = pstart[sorted_e] + jnp.arange(nk, dtype=jnp.int32) - start[sorted_e]
    n_blocks = (nk + N_EXPERTS * (EXPERT_BLOCK - 1) + EXPERT_BLOCK - 1) // EXPERT_BLOCK
    p_rows = n_blocks * EXPERT_BLOCK
    row_tok = jnp.full((p_rows,), n, jnp.int32).at[dest].set(flat_tok[order])
    row_gate = jnp.zeros((p_rows,), xf.dtype).at[dest].set(flat_g[order])
    block_start = jnp.arange(n_blocks, dtype=jnp.int32) * EXPERT_BLOCK
    block_e = jnp.minimum(jnp.searchsorted(pend, block_start, side="right"), N_EXPERTS - 1)
    x_pad = jnp.concatenate([xf, jnp.zeros((1, d), xf.dtype)], axis=0)

    def block_fn(args):
        tok, e, g = args
        xb = x_pad[tok]
        return swiglu(xb, w1[e], w3[e], w2[e]) * g[:, None]

    yb = lax.map(block_fn, (row_tok.reshape(n_blocks, EXPERT_BLOCK), block_e,
                            row_gate.reshape(n_blocks, EXPERT_BLOCK)))
    y = jax.ops.segment_sum(yb.reshape(p_rows, d), row_tok, num_segments=n + 1)
    return y[:n]

def moe(xf, router_w, router_b, w1, w3, w2, sw1, sw3, sw2):
    scores = jax.nn.sigmoid((xf @ router_w).astype(jnp.float32))
    _, idx = lax.top_k(scores + router_b.astype(jnp.float32), TOP_K)
    g = jnp.take_along_axis(scores, idx, axis=-1)
    g = g / (jnp.sum(g, axis=-1, keepdims=True) + 1e-20) * ROUTED_SCALE
    return routed_experts(xf, idx, g.astype(xf.dtype), w1, w3, w2) + swiglu(xf, sw1, sw3, sw2)

def setup_inputs(seed: int = 0) -> dict:
    key = jax.random.key(seed)
    k = jax.random.split(key, 26)
    d = D_MODEL

    def nrm(kk, shape, scale):
        return jax.random.normal(kk, shape, jnp.float32) * scale

    return {
        "x": nrm(k[0], (BATCH, SEQ, d), 1.0),
        "c": nrm(k[1], (BATCH, d), 1.0),
        "ctx": nrm(k[2], (BATCH, CTX_LEN, d), 1.0),
        "c_ctx": nrm(k[3], (d,), 1.0),
        "ada_w": nrm(k[4], (DEPTH, d, MOD_CHUNKS * d), 0.01),
        "ada_b": nrm(k[5], (DEPTH, MOD_CHUNKS * d), 0.02),
        "norm1_g": 1.0 + nrm(k[6], (DEPTH, d), 0.02),
        "norm2_g": 1.0 + nrm(k[7], (DEPTH, d), 0.02),
        "ev_w_in": nrm(k[8], (N_EVEN, d, EVEN_IN), d ** -0.5),
        "ev_w_s": nrm(k[9], (N_EVEN, GMLP_GROUPS, CHUNK, CHUNK), CHUNK ** -0.5),
        "ev_b_s": 1.0 + nrm(k[10], (N_EVEN, GMLP_GROUPS, CHUNK), 0.02),
        "ev_w_out": nrm(k[11], (N_EVEN, EVEN_MIX, d), EVEN_MIX ** -0.5),
        "od_w_in": nrm(k[12], (N_ODD, d, ODD_IN), d ** -0.5),
        "od_q_norm_g": 1.0 + nrm(k[13], (N_ODD, HEAD_DIM), 0.02),
        "od_k_norm_g": 1.0 + nrm(k[14], (N_ODD, HEAD_DIM), 0.02),
        "od_sink": nrm(k[15], (N_ODD, N_HEADS), 0.5),
        "od_conv_w": nrm(k[16], (N_ODD, CONV_WIDTH, D_CONV), CONV_WIDTH ** -0.5),
        "od_w_out": nrm(k[17], (N_ODD, ODD_MIX, d), ODD_MIX ** -0.5),
        "router_w": nrm(k[18], (DEPTH, d, N_EXPERTS), d ** -0.5),
        "router_b": nrm(k[19], (DEPTH, N_EXPERTS), 0.01),
        "exp_w_gate": nrm(k[20], (DEPTH, N_EXPERTS, d, D_EXPERT), d ** -0.5),
        "exp_w_up": nrm(k[21], (DEPTH, N_EXPERTS, d, D_EXPERT), d ** -0.5),
        "exp_w_down": nrm(k[22], (DEPTH, N_EXPERTS, D_EXPERT, d), D_EXPERT ** -0.5),
        "sh_w_gate": nrm(k[23], (DEPTH, d, D_SHARED), d ** -0.5),
        "sh_w_up": nrm(k[24], (DEPTH, d, D_SHARED), d ** -0.5),
        "sh_w_down": nrm(k[25], (DEPTH, D_SHARED, d), D_SHARED ** -0.5),
    }

def reference(x, c, ctx, c_ctx, ada_w, ada_b, norm1_g, norm2_g,
              ev_w_in, ev_w_s, ev_b_s, ev_w_out,
              od_w_in, od_q_norm_g, od_k_norm_g, od_sink, od_conv_w, od_w_out,
              router_w, router_b, exp_w_gate, exp_w_up, exp_w_down,
              sh_w_gate, sh_w_up, sh_w_down):
    b, s, d = x.shape
    lc = ctx.shape[1]
    cos, sin = axial_rope_tables(s)
    xc = ctx
    for l in range(DEPTH):
        last = l == DEPTH - 1
        even = l % 2 == 0
        need_ctx_mix = not (last and even)
        sh1, sc1, gt1, sh2, sc2, gt2 = modulation(c, ada_w[l], ada_b[l])
        h = modulate(rms_norm(x, norm1_g[l]), sh1, sc1)
        if need_ctx_mix:
            csh1, csc1, cgt1, csh2, csc2, cgt2 = modulation(c_ctx, ada_w[l], ada_b[l])
            hc = modulate(rms_norm(xc, norm1_g[l]), csh1, csc1)
        if even:
            e = l // 2
            y = even_mixer(h, ev_w_in[e], ev_w_s[e], ev_b_s[e], ev_w_out[e])
            yc = None if last else even_mixer(hc, ev_w_in[e], ev_w_s[e], ev_b_s[e], ev_w_out[e])
        else:
            o = l // 2
            y, yc = odd_mixer(h, hc, od_w_in[o], od_q_norm_g[o], od_k_norm_g[o], od_sink[o],
                              od_conv_w[o], od_w_out[o], cos, sin, not last)
        x = x + gt1 * y
        h2 = modulate(rms_norm(x, norm2_g[l]), sh2, sc2)
        moe_args = (router_w[l], router_b[l], exp_w_gate[l], exp_w_up[l], exp_w_down[l],
                    sh_w_gate[l], sh_w_up[l], sh_w_down[l])
        if last:
            x = x + gt2 * moe(h2.reshape(b * s, d), *moe_args).reshape(b, s, d)
        else:
            xc = xc + cgt1 * yc
            h2c = modulate(rms_norm(xc, norm2_g[l]), csh2, csc2)
            tokens = jnp.concatenate([h2.reshape(b * s, d), h2c.reshape(b * lc, d)], axis=0)
            out = moe(tokens, *moe_args)
            x = x + gt2 * out[:b * s].reshape(b, s, d)
            xc = xc + cgt2 * out[b * s:].reshape(b, lc, d)
    return x


_drawn_inputs = setup_inputs


def setup_inputs(seed=0):
    import zlib

    import numpy as np

    out = dict(_drawn_inputs(seed))
    spreads = {}
    factors = {'ctx': 4.28,
     'c_ctx': 2.861,
     'norm1_g': 3.633,
     'ev_b_s': 5.468,
     'od_q_norm_g': 49.982,
     'od_k_norm_g': 48.606,
     'od_sink': 8.0,
     'norm2_g': 3.302}
    for name, (base, spread) in spreads.items():
        noise = np.random.default_rng([zlib.crc32(name.encode()), seed]).standard_normal(out[name].shape)
        drawn = base * np.exp(spread * noise) if base else spread * noise
        out[name] = __import__('jax').numpy.asarray(drawn.astype(out[name].dtype))
    for name, factor in factors.items():
        out[name] = (out[name] * factor).astype(out[name].dtype)
    return out
```

```python
from contextlib import ExitStack

import numpy as np
import concourse.bass as bass
from concourse import mybir

F32, BF16, I32, U32 = mybir.dt.float32, mybir.dt.bfloat16, mybir.dt.int32, mybir.dt.uint32
ALU = mybir.AluOpType
ACT = mybir.ActivationFunctionType
AX = mybir.AxisListType
ds = bass.ds

P = 128
D = 1024
KT = D // P
SEQ, CTX = 1024, 256
LT, CT = SEQ // P, CTX // P
NT = LT + CT
TOK = SEQ + CTX
EPS = 1e-6
HALF = D // 2
EVEN_IN = 3 * HALF
HEADS, KVH, DH = 8, 2, 64
QW, KVW = HEADS * DH, KVH * DH
ODD_IN = QW + 2 * KVW + 3 * HALF
ROPE = DH // 4
NE, TOPK, DE = 64, 6, 256
SCALE_ROUTED = 2.5
MOD = 6 * D
BANK = 512
KEYS = 3 * P + CTX
MASKED = -1e30


def blocks_bound(tokens):
    n = (tokens * TOPK + NE * (P - 1)) // P
    return n + n % 2


NBLK = blocks_bound(TOK)
TABLE = NBLK + 3
DUMMY = TOK
SLOT = 2 * KT * DE + 2 * D


class Machine:

    def __init__(self, nc, ctx, io):
        self.nc, self.ctx, self.io, self.sems = nc, ctx, io, {}

        def sb(name, shape, dt=F32):
            return ctx.enter_context(nc.sbuf_tensor(name, shape, dt))

        self.ht = sb("ht", [P, KT * TOK])
        self.mx = sb("mx", [P, KT * TOK])
        self.w = sb("w", [P, 20480])
        self.bc = sb("bc", [P, 4 * D])
        self.gt = sb("gt", [P, 2 * D])
        self.st = sb("st", [P, 2 * D])
        self.kv = sb("kv", [P, NT * 2 * KVW])
        self.ident = sb("ident", [P, P])
        self.ones = sb("ones", [P, P], BF16)
        self.before = sb("before", [P, P], BF16)
        self.iota_e = sb("iota_e", [P, NE])
        self.iota_blk = sb("iota_blk", [P, 1])
        self.band = sb("band", [P, 3 * P])
        self.cond = sb("cond", [P, KT, 2])
        self.ss = sb("ss", [P, NT])
        self.rstd = sb("rstd", [P, NT])
        self.logits = self.kv[:, 0:NT * NE].rearrange("p (t e) -> p t e", e=NE)
        self.slots = sb("slots", [P, TABLE, 2], I32)
        self.index = self.kv[:, NT * NE:NT * NE + 4].bitcast(I32)
        self.regs = self.kv[0:1, 1024:1024 + 3 * P].bitcast(I32)
        self.ps = ctx.enter_context(nc.psum_tensor("ps", [P, 8 * BANK], F32))

        def dram(name, shape, dt=F32):
            return nc.dram_tensor(name, shape, dt).ap()

        self.modrow = dram("modrow", [2, 2, MOD])
        self.xres = dram("xres", [TOK, D])
        self.h2 = dram("h2", [TOK + P, D])
        self.y = dram("y", [TOK + P, D])
        self.slot_table = dram("slot_table", [TABLE * P, 2], I32)
        self.block_expert = dram("block_expert", [P, 1], I32)
        self.stage_done = self.sem("stage_done")

    def sem(self, name):
        if name not in self.sems:
            self.sems[name] = self.ctx.enter_context(self.nc.semaphore(name))
        return self.sems[name]

    def bank(self, n, cols=BANK):
        return self.ps[:, n * BANK:n * BANK + cols]

    def meet(self, eng, n):
        eng.drain().then_inc(self.stage_done, 1)
        eng.wait_ge(self.stage_done, 5 * n)


def wait_some(eng, sem, value):
    if not (isinstance(value, int) and value == 0):
        eng.wait_ge(sem, value)


def settle(eng, sem):
    eng.sem_inc(sem)


def bcast(row, parts=P):
    return row.partition_broadcast(parts)


def along(ap, axis, shape):
    return ap.unsqueeze(axis).broadcast_to(shape)


class Stage:
    def __init__(self, m):
        self.m, self.nc = m, m.nc
        self.mine = []

    def signals(self, stage, names):
        return [self.own(f"{stage}_{name}") for name in names.split()]

    def own(self, name):
        self.mine.append(self.m.sem(name))
        return self.mine[-1]

    def sync(self, sp):
        pass

    def pool(self, pool):
        pass

    def act(self, act):
        pass

    def dve(self, dve):
        pass

    def pe(self, pe):
        pass


class Setup(Stage):

    def __init__(self, m):
        super().__init__(m)
        self.made, self.loaded, self.stored = self.signals("setup", "made loaded stored")

    def sync(self, sp):
        m, io = self.m, self.m.io
        sp.dma_start(m.st[:, 0:KT], io["c"].rearrange("o (p k) -> (o p) k", k=KT)).then_inc(self.loaded, 16)
        sp.dma_start(m.st[:, KT:2 * KT], io["c_ctx"].rearrange("(p k) -> p k", k=KT)).then_inc(self.loaded, 16)
        sp.wait_ge(self.made, 1)
        sp.dma_start(m.h2[DUMMY:DUMMY + P, :], m.bc[:, 0:D]).then_inc(self.stored, 16)
        sp.dma_start(m.y[DUMMY:DUMMY + P, :], m.bc[:, 0:D]).then_inc(self.stored, 16)
        sp.wait_ge(self.stored, 32)

    def act(self, act):
        m = self.m
        act.wait_ge(self.loaded, 32)
        self.nc.scalar.activation(m.cond[:, :, :].rearrange("p k c -> p c k"),
                                  m.st[:, 0:2 * KT].rearrange("p (c k) -> p c k", c=2), ACT.Silu)

    def pool(self, pool):
        m, nc = self.m, self.nc
        g = nc.gpsimd
        g.memset(m.bc[:, 0:D], 0.0).then_inc(self.made, 1)
        g.memset(m.ident[:, :], 0.0)
        g.memset(m.ones[:, :], 1.0)
        g.memset(m.before[:, :], 1.0)
        g.memset(m.band[:, :], 0.0)
        g.iota(m.iota_e[:, :], [[1, NE]], base=0, channel_multiplier=0, allow_small_or_imprecise_dtypes=True)
        g.iota(m.iota_blk[:, :], [[0, 1]], base=0, channel_multiplier=P, allow_small_or_imprecise_dtypes=True)
        pool.drain()
        g.affine_select(out=m.ident[:, :], in_=m.ident[:, :], compare_op=ALU.not_equal, fill=1.0, base=0,
                        pattern=[[-1, P]], channel_multiplier=1)
        g.affine_select(out=m.before[:, :], in_=m.before[:, :], compare_op=ALU.is_gt, fill=0.0, base=0,
                        pattern=[[1, P]], channel_multiplier=-1)
        g.affine_select(out=m.band[:, 0:P], in_=m.band[:, 0:P], compare_op=ALU.is_ge, fill=MASKED, base=0,
                        pattern=[[1, P]], channel_multiplier=-1)
        g.affine_select(out=m.band[:, 2 * P:], in_=m.band[:, 2 * P:], compare_op=ALU.is_ge, fill=MASKED, base=0,
                        pattern=[[-1, P]], channel_multiplier=1)


class Modulation(Stage):

    CHUNKS = MOD // BANK
    RING = 5

    def __init__(self, m, layer):
        super().__init__(m)
        self.product, self.evacuated, self.ready, self.rows, self.stored = self.signals("mod", "product evacuated ready rows stored")
        self.layer = layer
        self.chunk = [self.own(f"mod_chunk{i}") for i in range(self.RING)]

    def wchunk(self, j):
        s = (j % self.RING) * KT * BANK
        return self.m.w[:, s:s + KT * BANK].rearrange("p (k n) -> p k n", k=KT)

    def sync(self, sp):
        m, io, L = self.m, self.m.io, self.layer
        w = io["ada_w"][L].rearrange("(p k) n -> p k n", k=KT)
        for j in range(self.CHUNKS):
            if j >= self.RING:
                sp.wait_ge(self.product, j - self.RING + 1)
            sp.dma_start(self.wchunk(j), w[:, :, j * BANK:(j + 1) * BANK]).then_inc(self.chunk[j % self.RING], 16)
            if j == 0:
                sp.dma_start(m.mx[0:2, 0:MOD], bcast(io["ada_b"][L], 2)).then_inc(self.rows, 16)
                sp.dma_start(m.mx[0:2, MOD:MOD + D], bcast(io["norm1_g"][L], 2)).then_inc(self.rows, 16)
                sp.dma_start(m.mx[0:2, MOD + D:MOD + 2 * D], bcast(io["norm2_g"][L], 2)).then_inc(self.rows, 16)
        sp.wait_ge(self.ready, 1)
        sp.dma_start(m.modrow[L], m.ht[0:2, 0:MOD]).then_inc(self.stored, 16)
        sp.wait_ge(self.stored, 16)

    def pe(self, pe):
        m = self.m
        for j in range(self.CHUNKS):
            pe.wait_ge(self.chunk[j % self.RING], 16 * (j // self.RING + 1))
            if j >= 4:
                pe.wait_ge(self.evacuated, j - 3)
            for k in range(KT):
                last = self.nc.tensor.matmul(m.bank(j % 4)[0:2, :], m.cond[:, k, :], self.wchunk(j)[:, k, :],
                                             start=(k == 0), stop=(k == KT - 1))
            last.then_inc(self.product, 1)

    def dve(self, dve):
        m, v = self.m, self.nc.vector
        row = m.ht[0:2, 0:MOD]
        dve.wait_ge(self.rows, 48)
        for j in range(self.CHUNKS):
            c = slice(j * BANK, (j + 1) * BANK)
            dve.wait_ge(self.product, j + 1)
            v.tensor_tensor(row[:, c], m.bank(j % 4)[0:2, :], m.mx[0:2, c], ALU.add).then_inc(self.evacuated, 1)
        dve.drain()
        for i, g in ((1, 0), (4, 1)):
            part = row[:, i * D:(i + 1) * D]
            last = v.scalar_tensor_tensor(part, part, 1.0, m.mx[0:2, MOD + g * D:MOD + (g + 1) * D], ALU.add, ALU.mult)
        last.then_inc(self.ready, 1)


class NormIn(Stage):

    def __init__(self, m, layer):
        super().__init__(m)
        self.mods, self.xfree, self.squared, self.varied, self.rooted = self.signals("in", "mods xfree squared varied rooted")
        self.hready, self.transposed, self.hta, self.htd, self.rows = self.signals("in", "hready transposed hta htd rows")
        self.rows_out, self.x_new = self.signals("in", "rows_out x_new")
        self.layer = layer
        self.xl = [self.own(f"in_x{i}") for i in range(2)]
        self.xs = [self.own(f"in_xs{i}") for i in range(2)]
        self.wl = self.own(f"in_w")
        if layer == 0:
            self.win, self.cols, self.tiles = EVEN_IN, [(HALF, HALF)], range(NT)
        else:
            self.win, self.cols, self.tiles = ODD_IN, [(0, QW), (QW, 2 * KVW)], range(NT)

    def weights(self):
        return self.m.w[:, 0:KT * self.win].rearrange("p (k n) -> p k n", k=KT)

    def parts(self, t):
        return self.cols if self.layer == 0 or t < LT else self.cols[1:]

    def row_out(self, t, i):
        m = self.m
        if self.layer == 0:
            return m.w[:, KT * EVEN_IN + t * HALF:KT * EVEN_IN + (t + 1) * HALF]
        if i == 0:
            return m.mx[:, t * QW:(t + 1) * QW]
        return m.kv[:, t * 2 * KVW:(t + 1) * 2 * KVW]

    def hrow(self, t):
        o = (4 + t % 2) * TOK
        return self.m.mx[:, o:o + D]

    def sync(self, sp):
        m, io, L = self.m, self.m.io, self.layer
        win = io["ev_w_in" if L == 0 else "od_w_in"][0].rearrange("(p k) n -> p k n", k=KT)
        for i, (row, seg) in enumerate(((0, 1), (0, 0), (1, 1), (1, 0))):
            sp.dma_start(m.bc[:, i * D:(i + 1) * D],
                         bcast(m.modrow[L, row, seg * D:(seg + 1) * D])).then_inc(self.mods, 16)
        if L:
            for row in range(2):
                sp.dma_start(m.gt[:, row * D:(row + 1) * D],
                             bcast(m.modrow[0, row, 5 * D:6 * D])).then_inc(self.mods, 16)
        for t in self.tiles:
            if t >= 2:
                sp.wait_ge(self.hready, t - 1)
                if L:
                    sp.wait_ge(self.xs[t % 2], 16 * (t // 2))
            tok = slice(t * P, (t + 1) * P)
            if L:
                src = m.xres[tok, :]
                sp.dma_start(self.yin(t), m.y[tok, :]).then_inc(self.xl[t % 2], 16)
            else:
                src = io["x"][0, tok, :] if t < LT else io["ctx"][0, t * P - SEQ:(t + 1) * P - SEQ, :]
            sp.dma_start(m.st[:, (t % 2) * D:(t % 2 + 1) * D], src).then_inc(self.xl[t % 2], 16)
            if t == 1:
                sp.dma_start(self.weights(), win).then_inc(self.wl, 16)
            if L and t >= 1:
                self.store_x(sp, t - 1)
        if L:
            self.store_x(sp, NT - 1)
            for i in range(2):
                sp.wait_ge(self.xs[i], 16 * NT // 2)

    def store_x(self, sp, t):
        m = self.m
        sp.wait_ge(self.x_new, t + 1)
        sp.dma_start(m.xres[t * P:(t + 1) * P, :],
                     m.st[:, (t % 2) * D:(t % 2 + 1) * D]).then_inc(self.xs[t % 2], 16)

    def yin(self, t):
        o = (6 + t % 2) * TOK
        return self.m.mx[:, o:o + D]

    def act(self, act):
        m, a = self.m, self.nc.scalar
        for t in range(NT + 2):
            if t < NT:
                x = m.st[:, (t % 2) * D:(t % 2 + 1) * D]
                if self.layer:
                    act.wait_ge(self.x_new, t + 1)
                else:
                    act.wait_ge(self.xl[t % 2], 16 * (t // 2 + 1))
                act.drain()
                a.activation(m.mx[:, LT * QW:LT * QW + D], x, ACT.Square, accum_out=m.ss[:, t:t + 1]).then_inc(self.squared, 1)
                act.wait_ge(self.varied, t + 1)
                a.activation(m.rstd[:, t:t + 1], m.rstd[:, t:t + 1], ACT.Sqrt).then_inc(self.rooted, 1)
            if 1 <= t <= NT:
                u = t - 1
                act.wait_ge(self.transposed, u + 1)
                a.copy(self.ht_part(u, 0), m.bank(2 * (u % 2)).rearrange("p (k n) -> p k n", k=4)).then_inc(self.hta, 1)
            if t >= 2:
                u = t - 2
                act.wait_ge(self.rows, u + 1)
                for i in range(2 - len(self.parts(u)), 2):
                    part = self.cols[i] if len(self.cols) == 2 else self.cols[0]
                    b = self.row_bank(u, i)
                    last = a.copy(self.row_out(u, i), m.bank(b, part[1]))
                last.then_inc(self.rows_out, 1)

    def row_bank(self, t, i):
        return 4 + 2 * (t % 2) + i

    def ht_part(self, t, half):
        m = self.m
        return m.ht[:, half * 4 * TOK:(half + 1) * 4 * TOK].rearrange("p (k n) -> p k n", k=4)[:, :, t * P:(t + 1) * P]

    def dve(self, dve):
        m, v = self.m, self.nc.vector
        dve.wait_ge(self.mods, 16 * (6 if self.layer else 4))
        for t in range(NT + 1):
            if t < NT:
                x = m.st[:, (t % 2) * D:(t % 2 + 1) * D]
                c = 0 if t < LT else 1
                if self.layer:
                    dve.wait_ge(self.xl[t % 2], 32 * (t // 2 + 1))
                    v.tensor_tensor(self.yin(t), self.yin(t), m.gt[:, c * D:(c + 1) * D], ALU.mult)
                    dve.drain()
                    v.tensor_tensor(x, x, self.yin(t), ALU.add).then_inc(self.x_new, 1)
                dve.wait_ge(self.squared, t + 1)
                v.tensor_scalar(m.rstd[:, t:t + 1], m.ss[:, t:t + 1], 1.0 / D, EPS, ALU.mult, ALU.add).then_inc(self.varied, 1)
                dve.wait_ge(self.rooted, t + 1)
                v.reciprocal(m.rstd[:, t:t + 1], m.rstd[:, t:t + 1])
                if t >= 2:
                    dve.wait_ge(self.transposed, t - 1)
                dve.drain()
                v.scalar_tensor_tensor(self.hrow(t), x, m.rstd[:, t:t + 1], m.bc[:, 2 * c * D:(2 * c + 1) * D],
                                       ALU.mult, ALU.mult)
                dve.drain()
                v.tensor_tensor(self.hrow(t), self.hrow(t), m.bc[:, (2 * c + 1) * D:(2 * c + 2) * D],
                                ALU.add).then_inc(self.hready, 1)
            if t >= 1:
                u = t - 1
                dve.wait_ge(self.transposed, u + 1)
                v.tensor_copy(self.ht_part(u, 1), m.bank(2 * (u % 2) + 1).rearrange("p (k n) -> p k n", k=4)).then_inc(self.htd, 1)

    def pe(self, pe):
        m, te = self.m, self.nc.tensor
        for t in range(NT + 1):
            if t < NT:
                pe.wait_ge(self.hready, t + 1)
                if t >= 2:
                    pe.wait_ge(self.hta, t - 1)
                    pe.wait_ge(self.htd, t - 1)
                transpose_rows(te, m, self.hrow(t), 2 * (t % 2)).then_inc(self.transposed, 1)
            if t >= 1:
                u = t - 1
                if u == 0:
                    pe.wait_ge(self.wl, 16)
                pe.wait_ge(self.hta, u + 1)
                pe.wait_ge(self.htd, u + 1)
                if u >= 2:
                    pe.wait_ge(self.rows_out, u - 1)
                for i in range(2 - len(self.parts(u)), 2):
                    c0, n = self.cols[i] if len(self.cols) == 2 else self.cols[0]
                    for k in range(KT):
                        last = te.matmul(m.bank(self.row_bank(u, i), n), m.ht[:, k * TOK + u * P:k * TOK + (u + 1) * P],
                                         self.weights()[:, k, c0:c0 + n], start=(k == 0), stop=(k == KT - 1))
                last.then_inc(self.rows, 1)


def transpose_rows(te, m, rows, bank):
    by_slab = rows.rearrange("p (c k) -> p k c", k=KT)
    for k in range(KT):
        last = te.transpose(m.ps[:, bank * BANK + k * P:bank * BANK + (k + 1) * P], by_slab[:, k, :], m.ident[:, :])
    return last


TOKEN_CHUNKS = [(0, 512), (512, 512), (1024, 256)]


class EvenProjections(Stage):

    def __init__(self, m):
        super().__init__(m)
        self.ws, self.wst, self.wst_sb, self.gelu_v, self.stats = self.signals("ev", "ws wst wst_sb gelu_v stats")
        self.std, self.vn, self.product, self.done, self.spatial = self.signals("ev", "std vn product done spatial")
        self.gated, self.bias = self.signals("ev", "gated bias")

    def sync(self, sp):
        m, io = self.m, self.m.io
        sp.dma_start(m.bc[:, 0:512].rearrange("p (g q) -> p g q", g=4),
                     io["ev_w_s"][0].rearrange("g p q -> p g q")).then_inc(self.ws, 16)
        sp.dma_start(m.st[:, 0:512], bcast(io["ev_b_s"][0].rearrange("g p -> (g p)"))).then_inc(self.bias, 16)

    def v_rows(self):
        m = self.m
        return m.w[:, KT * EVEN_IN:KT * EVEN_IN + NT * HALF]

    def chunks(self):
        for cols in (0, 2 * HALF):
            for i in range(4):
                for c0, n in TOKEN_CHUNKS:
                    yield cols + i * P, (i if cols == 0 else 4 + i), c0, n

    def pe(self, pe):
        m, te = self.m, self.nc.tensor
        w = m.w[:, 0:KT * EVEN_IN].rearrange("p (k n) -> p k n", k=KT)
        pe.wait_ge(self.ws, 16)
        for g in range(4):
            last = te.transpose(m.bank(7)[:, g * P:(g + 1) * P], m.bc[:, g * P:(g + 1) * P], m.ident[:, :])
        last.then_inc(self.wst, 1)
        for q, (col, _, c0, n) in enumerate(self.chunks()):
            if q >= 6:
                pe.wait_ge(self.done, q - 5)
            for k in range(KT):
                last = te.matmul(m.bank(q % 6, n), w[:, k, col:col + P], m.ht[:, k * TOK + c0:k * TOK + c0 + n],
                                 start=(k == 0), stop=(k == KT - 1))
            last.then_inc(self.product, 1)
        pe.wait_ge(self.vn, 1)
        pe.wait_ge(self.wst_sb, 1)
        for t in range(NT):
            if t >= 2:
                pe.wait_ge(self.gated, t - 1)
            for g in range(4):
                last = te.matmul(m.bank(6 + t % 2)[:, g * P:(g + 1) * P],
                                 self.v_rows()[:, t * HALF + g * P:t * HALF + (g + 1) * P],
                                 m.bc[:, 512 + g * P:512 + (g + 1) * P], start=True, stop=True)
            last.then_inc(self.spatial, 1)

    def act(self, act):
        m, a = self.m, self.nc.scalar
        a.activation(self.v_rows(), self.v_rows(), ACT.Gelu_apprx_tanh).then_inc(self.gelu_v, 1)
        for q, (_, slab, c0, n) in enumerate(self.chunks()):
            if q == 12:
                act.wait_ge(self.stats, 1)
                a.activation(m.bc[:, 1024:1024 + 4 * NT], m.bc[:, 1024:1024 + 4 * NT], ACT.Sqrt).then_inc(self.std, 1)
            act.wait_ge(self.product, q + 1)
            dst = m.mx[:, slab * TOK + c0:slab * TOK + c0 + n]
            if slab < 4:
                ins = a.activation(dst, m.bank(q % 6, n), ACT.Gelu_apprx_tanh)
            else:
                ins = a.copy(dst, m.bank(q % 6, n))
            ins.then_inc(self.done, 1)

    def dve(self, dve):
        m, v = self.m, self.nc.vector
        G = 4 * NT
        dve.wait_ge(self.wst, 1)
        v.tensor_copy(m.bc[:, 512:1024], m.bank(7)).then_inc(self.wst_sb, 1)
        std, stats, mean = m.bc[:, 1024:1024 + G], m.bc[:, 1088:1088 + 6 * G], m.bc[:, 1408:1408 + 2 * G]
        dve.wait_ge(self.gelu_v, 1)
        for i in range(G):
            v.bn_stats(stats[:, 6 * i:6 * i + 6], self.v_rows()[:, i * P:(i + 1) * P])
        dve.drain()
        for i in range(G):
            v.bn_aggr(mean[:, 2 * i:2 * i + 2], stats[:, 6 * i:6 * i + 6])
        dve.drain()
        v.tensor_scalar(std, mean.rearrange("p (i c) -> p i c", c=2)[:, :, 1], 1e-5, None, ALU.add).then_inc(self.stats, 1)
        dve.wait_ge(self.std, 1)
        v.reciprocal(std, std)
        dve.drain()
        for i in range(G):
            part = self.v_rows()[:, i * P:(i + 1) * P]
            last = v.tensor_scalar(part, part, mean[:, 2 * i:2 * i + 1], std[:, i:i + 1], ALU.subtract, ALU.mult)
        last.then_inc(self.vn, 1)
        dve.wait_ge(self.bias, 16)
        dve.wait_ge(self.done, 24)
        bias = m.st[:, 0:512].rearrange("p (g n) -> p g n", g=4)
        for t in range(NT):
            tmp = m.st[:, 512 + (t % 2) * 512:1024 + (t % 2) * 512].rearrange("p (g n) -> p g n", g=4)
            u = m.mx[:, 0:4 * TOK].rearrange("p (g n) -> p g n", g=4)[:, :, t * P:(t + 1) * P]
            dve.wait_ge(self.spatial, t + 1)
            v.tensor_tensor(tmp, m.bank(6 + t % 2).rearrange("p (g n) -> p g n", g=4), bias, ALU.add).then_inc(self.gated, 1)
            dve.drain()
            v.tensor_tensor(u, u, tmp, ALU.mult)


class Fourier(Stage):

    H = SEQ // 2

    def __init__(self, m):
        super().__init__(m)
        self.tables, self.channel, self.spread_a, self.spread_d, self.cosine = self.signals("fft", "tables channel spread_a spread_d cosine")
        self.sine, self.sin_sb, self.folded, self.ctx_sum, self.ctx_out = self.signals("fft", "sine sin_sb folded ctx_sum ctx_out")

    def sync(self, sp):
        m, io = self.m, self.m.io
        w = m.w
        sp.dma_start(w[:, 0:256], io["dft_channel"]).then_inc(self.tables, 16)
        sp.dma_start(w[:, 256:256 + LT * 1024], io["dft_seq"]).then_inc(self.tables, 16)
        sp.dma_start(w[:, 8448:8448 + LT], io["dft_mid"]).then_inc(self.tables, 16)
        sp.dma_start(w[:, 8704:8704 + CT * 512], io["dft_ctx"]).then_inc(self.tables, 16)

    def spectrum(self, t):
        return self.m.ht[:, t * 1024:(t + 1) * 1024]

    def pe(self, pe):
        m, te = self.m, self.nc.tensor
        pe.wait_ge(self.tables, 64)
        for t in range(NT):
            if t >= 2:
                pe.wait_ge(self.spread_a, t - 1)
                pe.wait_ge(self.spread_d, t - 1)
            b = 2 * (t % 2) * BANK
            for g in range(4):
                last = te.matmul(m.ps[:, b + g * 256:b + (g + 1) * 256],
                                 m.mx[:, (4 + g) * TOK + t * P:(4 + g) * TOK + (t + 1) * P], m.w[:, 0:256],
                                 start=True, stop=True)
            last.then_inc(self.channel, 1)
        pe.wait_ge(self.spread_a, NT)
        pe.wait_ge(self.spread_d, NT)
        seq = m.w[:, 256:256 + LT * 1024].rearrange("p (t s n) -> p t s n", t=LT, s=2)
        for g in range(4):
            b = 3 * (g % 2)
            if g >= 2:
                pe.wait_ge(self.folded, g - 1)
            for t in range(LT):
                last = te.matmul(m.bank(b + 1), self.spectrum(t)[:, g * 256 + P:(g + 1) * 256], seq[:, t, 1, :],
                                 start=(t == 0), stop=(t == LT - 1))
            last.then_inc(self.sine, 1)
            for t in range(LT):
                te.matmul(m.bank(b), self.spectrum(t)[:, g * 256:g * 256 + P], seq[:, t, 0, :],
                          start=(t == 0), stop=(t == LT - 1))
            for t in range(LT):
                last = te.matmul(m.bank(b + 2, 1), self.spectrum(t)[:, g * 256:g * 256 + P],
                                 m.w[:, 8448 + t:8449 + t], start=(t == 0), stop=(t == LT - 1))
            last.then_inc(self.cosine, 1)
        small = m.w[:, 8704:8704 + CT * 512].rearrange("p (t s n) -> p t s n", t=CT, s=2)
        for g in range(4):
            if g >= 2:
                pe.wait_ge(self.ctx_out, g - 1)
            for i in range(2 * CT):
                t, s = divmod(i, 2)
                last = te.matmul(m.bank(6 + g % 2, CTX), self.spectrum(LT + t)[:, g * 256 + s * P:g * 256 + (s + 1) * P],
                                 small[:, t, s, :], start=(i == 0), stop=(i == 2 * CT - 1))
            last.then_inc(self.ctx_sum, 1)

    def act(self, act):
        m, a = self.m, self.nc.scalar
        for t in range(NT):
            act.wait_ge(self.channel, t + 1)
            a.copy(self.spectrum(t)[:, 0:512], m.bank(2 * (t % 2))).then_inc(self.spread_a, 1)
        for g in range(4):
            act.wait_ge(self.sine, g + 1)
            if g >= 2:
                act.wait_ge(self.folded, g - 1)
            a.copy(m.st[:, (g % 2) * 512:(g % 2 + 1) * 512], m.bank(3 * (g % 2) + 1)).then_inc(self.sin_sb, 1)
        for g in range(4):
            act.wait_ge(self.ctx_sum, g + 1)
            a.copy(m.mx[:, (4 + g) * TOK + SEQ:(5 + g) * TOK], m.bank(6 + g % 2, CTX)).then_inc(self.ctx_out, 1)

    def dve(self, dve):
        m, v, H = self.m, self.nc.vector, self.H
        for t in range(NT):
            dve.wait_ge(self.channel, t + 1)
            v.tensor_copy(self.spectrum(t)[:, 512:1024], m.bank(2 * (t % 2) + 1)).then_inc(self.spread_d, 1)
        for g in range(4):
            out = m.mx[:, (4 + g) * TOK:(4 + g) * TOK + SEQ]
            cosines, sines = m.bank(3 * (g % 2)), m.st[:, (g % 2) * 512:(g % 2 + 1) * 512]
            dve.wait_ge(self.cosine, g + 1)
            dve.wait_ge(self.sin_sb, g + 1)
            v.tensor_tensor(out[:, 0:H], cosines, sines, ALU.subtract)
            v.tensor_copy(out[:, H:H + 1], m.bank(3 * (g % 2) + 2, 1))
            v.tensor_tensor(out[:, SEQ - 1:H:-1], cosines[:, 1:H], sines[:, 1:H], ALU.add).then_inc(self.folded, 1)


class MixOut(Stage):

    def __init__(self, m, layer, tiles):
        super().__init__(m)
        self.mods, self.wl, self.product, self.gated_y, self.x_new = self.signals("out", "mods wl product gated_y x_new")
        self.squared, self.varied, self.rooted, self.hready, self.transposed = self.signals("out", "squared varied rooted hready transposed")
        self.hta, self.htd, self.logit, self.logit_out = self.signals("out", "hta htd logit logit_out")
        self.layer, self.tiles = layer, tiles
        self.xl = [self.own(f"out_x{i}") for i in range(2)]
        self.xs = [self.own(f"out_s{i}") for i in range(2)]
        self.hs = [self.own(f"out_h{i}") for i in range(2)]

    W_ROUTER = KT * D
    W_HROW = W_ROUTER + KT * NE
    W_Y = W_HROW + 2 * D
    W_JUNK = W_Y + 2 * D

    def hrow(self, t):
        return self.m.w[:, self.W_HROW + (t % 2) * D:self.W_HROW + (t % 2 + 1) * D]

    def ytmp(self, t):
        return self.m.w[:, self.W_Y + (t % 2) * D:self.W_Y + (t % 2 + 1) * D]

    def x(self, t):
        return self.m.st[:, (t % 2) * D:(t % 2 + 1) * D]

    def load_weights(self, sp):
        m, io, L = self.m, self.m.io, self.layer
        wout = io["ev_w_out" if L == 0 else "od_w_out"][0].rearrange("(k p) n -> p k n", p=P)
        sp.dma_start(m.w[:, 0:KT * D].rearrange("p (k n) -> p k n", k=KT), wout).then_inc(self.wl, 16)
        sp.dma_start(m.w[:, self.W_ROUTER:self.W_HROW].rearrange("p (k n) -> p k n", k=KT),
                     io["router_w"][L].rearrange("(p k) n -> p k n", k=KT)).then_inc(self.wl, 16)

    def sync(self, sp):
        m, io, L = self.m, self.m.io, self.layer
        self.load_weights(sp)
        for i, (row, seg) in enumerate(((0, 4), (0, 3), (1, 4), (1, 3))):
            sp.dma_start(m.bc[:, i * D:(i + 1) * D],
                         bcast(m.modrow[L, row, seg * D:(seg + 1) * D])).then_inc(self.mods, 16)
        for row in range(2):
            sp.dma_start(m.gt[:, row * D:(row + 1) * D],
                         bcast(m.modrow[L, row, 2 * D:3 * D])).then_inc(self.mods, 16)
        n = self.tiles
        for t in range(n + 1):
            if t < n:
                tok = slice(t * P, (t + 1) * P)
                if t >= 2:
                    sp.wait_ge(self.hready, t - 1)
                    sp.wait_ge(self.xs[t % 2], 16 * (t // 2))
                if L:
                    src = m.xres[tok, :]
                else:
                    src = io["x"][0, tok, :] if t < LT else io["ctx"][0, t * P - SEQ:(t + 1) * P - SEQ, :]
                sp.dma_start(self.x(t), src).then_inc(self.xl[t % 2], 16)
            if t >= 1:
                u = t - 1
                tok = slice(u * P, (u + 1) * P)
                sp.wait_ge(self.x_new, u + 1)
                sp.dma_start(m.xres[tok, :], self.x(u)).then_inc(self.xs[u % 2], 16)
                sp.wait_ge(self.hready, u + 1)
                sp.dma_start(m.h2[tok, :], self.hrow(u)).then_inc(self.hs[u % 2], 16)
        for i in range(2):
            sp.wait_ge(self.xs[i], 8 * n)
            sp.wait_ge(self.hs[i], 8 * n)

    def act(self, act):
        m, a = self.m, self.nc.scalar
        n = self.tiles
        for t in range(n + 2):
            if t < n:
                act.wait_ge(self.x_new, t + 1)
                act.drain()
                a.activation(m.w[:, self.W_JUNK:self.W_JUNK + D], self.x(t), ACT.Square,
                             accum_out=m.ss[:, t:t + 1]).then_inc(self.squared, 1)
                act.wait_ge(self.varied, t + 1)
                a.activation(m.rstd[:, t:t + 1], m.rstd[:, t:t + 1], ACT.Sqrt).then_inc(self.rooted, 1)
            if 1 <= t <= n:
                u = t - 1
                act.wait_ge(self.transposed, u + 1)
                a.copy(self.ht_part(u, 0), m.bank(4).rearrange("p (k n) -> p k n", k=4)).then_inc(self.hta, 1)
            if t >= 2:
                u = t - 2
                act.wait_ge(self.logit, u + 1)
                a.copy(m.logits[:, u, :], m.bank(6 + u % 2, NE)).then_inc(self.logit_out, 1)

    def ht_part(self, t, half):
        m = self.m
        return m.ht[:, half * 4 * TOK:(half + 1) * 4 * TOK].rearrange("p (k n) -> p k n", k=4)[:, :, t * P:(t + 1) * P]

    def dve(self, dve):
        m, v = self.m, self.nc.vector
        n = self.tiles
        dve.wait_ge(self.mods, 96)
        for t in range(n + 1):
            if t < n:
                c = 0 if t < LT else 1
                dve.wait_ge(self.product, t + 1)
                b = 2 * (t % 2) * BANK
                v.tensor_tensor(self.ytmp(t), m.ps[:, b:b + D], m.gt[:, c * D:(c + 1) * D], ALU.mult).then_inc(self.gated_y, 1)
                dve.wait_ge(self.xl[t % 2], 16 * (t // 2 + 1))
                dve.drain()
                v.tensor_tensor(self.x(t), self.x(t), self.ytmp(t), ALU.add).then_inc(self.x_new, 1)
                dve.wait_ge(self.squared, t + 1)
                v.tensor_scalar(m.rstd[:, t:t + 1], m.ss[:, t:t + 1], 1.0 / D, EPS, ALU.mult, ALU.add).then_inc(self.varied, 1)
                dve.wait_ge(self.rooted, t + 1)
                v.reciprocal(m.rstd[:, t:t + 1], m.rstd[:, t:t + 1])
                if t >= 2:
                    dve.wait_ge(self.transposed, t - 1)
                    dve.wait_ge(self.hs[t % 2], 16 * (t // 2))
                dve.drain()
                v.scalar_tensor_tensor(self.hrow(t), self.x(t), m.rstd[:, t:t + 1], m.bc[:, 2 * c * D:(2 * c + 1) * D],
                                       ALU.mult, ALU.mult)
                dve.drain()
                v.tensor_tensor(self.hrow(t), self.hrow(t), m.bc[:, (2 * c + 1) * D:(2 * c + 2) * D],
                                ALU.add).then_inc(self.hready, 1)
            if t >= 1:
                u = t - 1
                dve.wait_ge(self.transposed, u + 1)
                v.tensor_copy(self.ht_part(u, 1), m.bank(5).rearrange("p (k n) -> p k n", k=4)).then_inc(self.htd, 1)

    def pe(self, pe):
        m, te = self.m, self.nc.tensor
        n = self.tiles
        pe.wait_ge(self.wl, 32)
        wout = m.w[:, 0:KT * D].rearrange("p (k n) -> p k n", k=KT)
        router = m.w[:, self.W_ROUTER:self.W_HROW].rearrange("p (k n) -> p k n", k=KT)
        for t in range(n + 2):
            if t < n:
                if t >= 2:
                    pe.wait_ge(self.gated_y, t - 1)
                for h in range(2):
                    for k in range(KT):
                        last = te.matmul(m.bank(2 * (t % 2) + h), m.mx[:, k * TOK + t * P:k * TOK + (t + 1) * P],
                                         wout[:, k, h * BANK:(h + 1) * BANK], start=(k == 0), stop=(k == KT - 1))
                last.then_inc(self.product, 1)
            if t >= 2:
                u = t - 2
                pe.wait_ge(self.hta, u + 1)
                pe.wait_ge(self.htd, u + 1)
                if u >= 2:
                    pe.wait_ge(self.logit_out, u - 1)
                for k in range(KT):
                    last = te.matmul(m.bank(6 + u % 2, NE), m.ht[:, k * TOK + u * P:k * TOK + (u + 1) * P],
                                     router[:, k, :], start=(k == 0), stop=(k == KT - 1))
                last.then_inc(self.logit, 1)
            if 1 <= t <= n:
                u = t - 1
                pe.wait_ge(self.hready, u + 1)
                if u >= 1:
                    pe.wait_ge(self.hta, u)
                    pe.wait_ge(self.htd, u)
                transpose_rows(te, m, self.hrow(u), 4).then_inc(self.transposed, 1)


class OddProjections(Stage):

    ROPE_AT = KT * ODD_IN
    GAIN_AT = ROPE_AT + 2 * LT * 2 * ROPE
    STD_AT = GAIN_AT + 2 * DH
    NSTD = LT * HEADS + NT * KVH
    CONV_AT = STD_AT + NSTD
    QTMP_AT = 20480 - 2 * QW

    def __init__(self, m):
        super().__init__(m)
        self.tables, self.means, self.std, self.product, self.gin_out = self.signals("odd", "tables means std product gin_out")
        self.z_out, self.out_done, self.padded = self.signals("odd", "z_out out_done padded")

    def sync(self, sp):
        m, io = self.m, self.m.io
        n = LT * 2 * ROPE
        sp.dma_start(m.w[:, self.ROPE_AT:self.ROPE_AT + 2 * n], io["rope"]).then_inc(self.tables, 16)
        sp.dma_start(m.w[:, self.GAIN_AT:self.GAIN_AT + DH], bcast(io["od_q_norm_g"][0])).then_inc(self.tables, 16)
        sp.dma_start(m.w[:, self.GAIN_AT + DH:self.GAIN_AT + 2 * DH], bcast(io["od_k_norm_g"][0])).then_inc(self.tables, 16)
        for j in range(3):
            sp.dma_start(m.w[:, self.CONV_AT + 4 * j:self.CONV_AT + 4 * j + 4],
                         io["od_conv_w"][0, j, :].rearrange("(m c) -> c m", c=P),
                         allow_slow_non_contiguous=True).then_inc(self.tables, 16)

    def products(self):
        base = QW + 2 * KVW
        for i in range(4):
            for part in (0, 2 * HALF, HALF):
                for half in range(2):
                    yield i, part, base + part + i * P, half

    def bank_of(self, n):
        return n % 8

    def pe(self, pe):
        m, te = self.m, self.nc.tensor
        w = m.w[:, 0:KT * ODD_IN].rearrange("p (k n) -> p k n", k=KT)
        users = (self.gin_out, self.z_out, self.out_done)
        for n, (_, _, col, half) in enumerate(self.products()):
            if n >= 8:
                i, j = divmod(n - 8, 6)
                pe.wait_ge(users[j // 2], 2 * i + j % 2 + 1)
            for k in range(KT):
                last = te.matmul(m.bank(n % 8), w[:, k, col:col + P],
                                 m.ht[:, k * TOK + half * BANK:k * TOK + (half + 1) * BANK],
                                 start=(k == 0), stop=(k == KT - 1))
            last.then_inc(self.product, 1)

    def act(self, act):
        m, a = self.m, self.nc.scalar
        std = m.w[:, self.STD_AT:self.STD_AT + self.NSTD]
        act.wait_ge(self.means, 1)
        a.activation(std, std, ACT.Sqrt).then_inc(self.std, 1)
        for i in range(4):
            for half in range(2):
                n = 6 * i + half
                act.wait_ge(self.product, n + 1)
                if i:
                    act.wait_ge(self.z_out, 2 * i)
                a.copy(m.st[:, half * BANK:(half + 1) * BANK], m.bank(n % 8)).then_inc(self.gin_out, 1)

    def dve(self, dve):
        m, v = self.m, self.nc.vector
        zc, yc, gin = m.gt[:, 0:SEQ + 2], m.st[:, D:2 * D], m.st[:, 0:D]
        v.memset(m.gt[:, 0:SEQ + 2], 0.0)
        q = m.mx[:, 0:LT * QW].rearrange("p (h d) -> p h d", d=DH)
        k = m.kv[:, :].rearrange("p (t c) -> p t c", t=NT)[:, :, 0:KVW].rearrange("p t (h d) -> p t h d", d=DH)
        std = m.w[:, self.STD_AT:self.STD_AT + self.NSTD]
        qstd, kstd = std[:, 0:LT * HEADS], std[:, LT * HEADS:].rearrange("p (t h) -> p t h", h=KVH)
        square = m.bc[:, 0:LT * QW].rearrange("p (h d) -> p h d", d=DH)
        v.tensor_tensor(square, q, q, ALU.mult)
        dve.drain()
        v.tensor_reduce(qstd, square, AX.X, ALU.add)
        dve.drain()
        square = m.bc[:, 0:NT * KVW].rearrange("p (t h d) -> p t h d", t=NT, d=DH)
        v.tensor_tensor(square, k, k, ALU.mult)
        dve.drain()
        v.tensor_reduce(kstd, square, AX.X, ALU.add)
        dve.drain()
        v.tensor_scalar(std, std, 1.0 / DH, EPS, ALU.mult, ALU.add).then_inc(self.means, 1)
        dve.wait_ge(self.std, 1)
        v.reciprocal(std, std)
        dve.drain()
        v.tensor_tensor(q, q, along(qstd, 2, [P, LT * HEADS, DH]), ALU.mult)
        v.tensor_tensor(k, k, along(kstd, 3, [P, NT, KVH, DH]), ALU.mult)
        dve.wait_ge(self.tables, 96)
        dve.drain()
        gain = m.w[:, self.GAIN_AT:self.GAIN_AT + 2 * DH]
        v.tensor_tensor(q, q, along(gain[:, 0:DH], 1, [P, LT * HEADS, DH]), ALU.mult)
        v.tensor_tensor(k, k, gain[:, DH:].unsqueeze(1).unsqueeze(1).broadcast_to([P, NT, KVH, DH]), ALU.mult)
        for t in range(LT):
            self.turn(dve, t)
        for i in range(4):
            self.conv(dve, i, zc, yc, gin)

    def turn(self, dve, t):
        m, v = self.m, self.nc.vector
        tables = m.w[:, self.ROPE_AT:self.GAIN_AT].rearrange("p (s t a f) -> p s t a f", s=2, t=LT, f=ROPE)
        jobs = []
        for src, dst, heads, tmp in (
                (m.mx[:, t * QW:(t + 1) * QW], m.bc[:, t * QW:(t + 1) * QW], HEADS, m.w[:, self.QTMP_AT:20480]),
                (m.kv[:, t * 2 * KVW:t * 2 * KVW + KVW], m.kv[:, t * 2 * KVW:t * 2 * KVW + KVW], KVH,
                 m.gt[:, 1100:1100 + 2 * KVW])):
            cut = "p (h a s f) -> p h a s f"
            src, dst = (x.rearrange(cut, a=2, s=2, f=ROPE) for x in (src, dst))
            c, s = (along(tables[:, i, t], 1, [P, heads, 2, ROPE]) for i in range(2))
            n = heads * 2 * ROPE
            a, b, c1, d = (tmp[:, i * n:(i + 1) * n].rearrange("p (h a f) -> p h a f", a=2, f=ROPE) for i in range(4))
            jobs.append((src, dst, c, s, a, b, c1, d))
        dve.drain()
        for src, dst, c, s, a, b, c1, d in jobs:
            x1, x2 = src[:, :, :, 0, :], src[:, :, :, 1, :]
            v.tensor_tensor(a, x1, c, ALU.mult)
            v.tensor_tensor(b, x2, s, ALU.mult)
            v.tensor_tensor(c1, x2, c, ALU.mult)
            v.tensor_tensor(d, x1, s, ALU.mult)
        dve.drain()
        for src, dst, c, s, a, b, c1, d in jobs:
            v.tensor_tensor(dst[:, :, :, 0, :], a, b, ALU.subtract)
            v.tensor_tensor(dst[:, :, :, 1, :], c1, d, ALU.add)

    def conv(self, dve, i, zc, yc, gin):
        m, v = self.m, self.nc.vector
        w = m.w[:, self.CONV_AT:self.CONV_AT + 12]
        for half in range(2):
            n = 6 * i + 2 + half
            dve.wait_ge(self.gin_out, 2 * i + half + 1)
            dve.wait_ge(self.product, n + 1)
            if half == 0:
                dve.drain()
            v.tensor_tensor(zc[:, 1 + half * BANK:1 + (half + 1) * BANK], gin[:, half * BANK:(half + 1) * BANK],
                            m.bank(n % 8), ALU.mult).then_inc(self.z_out, 1)
        dve.drain()
        v.tensor_scalar(yc, zc[:, 0:SEQ], w[:, i:i + 1], None, ALU.mult)
        for j in (1, 2):
            dve.drain()
            v.scalar_tensor_tensor(yc, zc[:, j:j + SEQ], w[:, 4 * j + i:4 * j + i + 1], yc, ALU.mult, ALU.add)
        dve.drain()
        for half in range(2):
            n = 6 * i + 4 + half
            dve.wait_ge(self.product, n + 1)
            c = slice(half * BANK, (half + 1) * BANK)
            v.tensor_tensor(m.mx[:, (4 + i) * TOK + half * BANK:(4 + i) * TOK + (half + 1) * BANK], yc[:, c],
                            m.bank(n % 8), ALU.mult).then_inc(self.out_done, 1)


class Attention(Stage):

    PAIRS = HEADS // KVH
    KCOLS = (LT + 2) * P + CTX
    V_AT = KVH * KCOLS
    S_AT = V_AT + (LT + 2 + CT) * KVW
    Q_AT = S_AT + 2 * 2 * KEYS
    PT_AT = 8704
    OROW_AT = PT_AT + 2 * 2 * KEYS
    MASK_AT = OROW_AT + 2 * QW
    SMALL_AT = MASK_AT + 3 * 3 * P

    def __init__(self, m):
        super().__init__(m)
        self.sink, self.padded, self.kt_made, self.keys_sb, self.q_row = self.signals("att", "sink padded kt_made keys_sb q_row")
        self.q_t, self.q_sb, self.scored, self.unloaded, self.maxed = self.signals("att", "q_t q_sb scored unloaded maxed")
        self.exped, self.turned, self.pt_sb, self.product, self.o_sb = self.signals("att", "exped turned pt_sb product o_sb")
        self.o_t, self.o_out, self.pe_settled = self.signals("att", "o_t o_out pe_settled")

    def s_buf(self, s):
        return self.m.ht[:, self.S_AT + s * 2 * KEYS:self.S_AT + (s + 1) * 2 * KEYS].rearrange("p (h c) -> p h c", h=2)

    def q_t_buf(self, tp):
        return self.m.ht[0:DH, self.Q_AT + tp * D:self.Q_AT + (tp + 1) * D]

    def pt(self, s):
        return self.m.w[:, self.PT_AT + s * 2 * KEYS:self.PT_AT + (s + 1) * 2 * KEYS]

    def orow(self, tp):
        return self.m.w[:, self.OROW_AT + tp * QW:self.OROW_AT + (tp + 1) * QW]

    def small(self, s, i):
        o = self.SMALL_AT + 16 + s * 16 + 2 * i
        return self.m.w[:, o:o + 2]

    def negated_sink(self):
        return self.m.w[:, self.SMALL_AT:self.SMALL_AT + HEADS]

    def key_columns(self, g):
        return self.m.ht[0:DH, g * self.KCOLS:(g + 1) * self.KCOLS]

    def v_rows(self):
        return self.m.ht[:, self.V_AT:self.S_AT]

    def tiles(self, eng, body):
        body(0, 0, 0)
        with eng.Fori(0, (LT - 2) // 2) as u:
            for half in range(2):
                body(2 * u + (1 + half), 1 - half, 1 + half)
        body(LT - 1, (LT - 1) % 2, LT - 1)

    def sync(self, sp):
        m, io = self.m, self.m.io
        sp.dma_start(self.negated_sink(), bcast(io["od_sink"][0])).then_inc(self.sink, 16)

    def pool(self, pool):
        m, g = self.m, self.nc.gpsimd
        for h in range(KVH):
            g.memset(m.ht[0:DH, h * self.KCOLS:h * self.KCOLS + P], 0.0)
            g.memset(m.ht[0:DH, h * self.KCOLS + (LT + 1) * P:h * self.KCOLS + (LT + 2) * P], 0.0)
        vr = self.v_rows().rearrange("p (t c) -> p t c", c=KVW)
        g.memset(vr[:, 0, :], 0.0)
        g.memset(vr[:, LT + 1, :], 0.0)
        kv = m.kv[:, :].rearrange("p (t c) -> p t c", t=NT)
        g.tensor_copy(vr[:, 1:LT + 1, :], kv[:, 0:LT, KVW:])
        g.tensor_copy(vr[:, LT + 2:, :], kv[:, LT:, KVW:])
        masks = m.w[:, self.MASK_AT:self.SMALL_AT].rearrange("p (i c) -> p i c", i=3)
        for i in range(3):
            g.tensor_copy(masks[:, i, :], m.band[:, :])
        pool.drain()
        g.memset(masks[:, 0, 0:P], MASKED)
        g.memset(masks[:, 2, 2 * P:], MASKED)
        pool.drain()
        g.memset(m.gt[:, 1024:1025], 0.0).then_inc(self.padded, 1)
        for t in range(2):
            g.tensor_copy(m.gt[:, t * QW:(t + 1) * QW], m.bc[:, t * QW:(t + 1) * QW]).then_inc(self.q_row, 1)
        with pool.Fori(0, (LT - 2) // 2) as u:
            for half in range(2):
                t = 2 * u + (2 + half)
                pool.wait_ge(self.q_t, 4 * u + 2 * (half + 1))
                g.tensor_copy(m.gt[:, half * QW:(half + 1) * QW], m.bc[:, ds(t * QW, QW)]).then_inc(self.q_row, 1)

    def transpose_q(self, pe, t, tp, half):
        m, te = self.m, self.nc.tensor
        pe.wait_ge(self.q_row, t + 1)
        settle(pe, self.pe_settled)
        for k in range(4):
            h = 4 * half + k
            last = te.transpose(m.ps[0:DH, 6 * BANK + k * P:6 * BANK + (k + 1) * P],
                                m.gt[:, tp * QW + h * DH:tp * QW + (h + 1) * DH], m.ident[:, :])
        last.then_inc(self.q_t, 1)

    def scores(self, pe, t, tp, j):
        m, te = self.m, self.nc.tensor
        settle(pe, self.pe_settled)
        for h in range(2):
            q = self.q_t_buf(tp)[:, (j + 4 * h) * P:(j + 4 * h + 1) * P]
            te.matmul(m.bank(h, 3 * P), q, m.ht[0:DH, ds(h * self.KCOLS + t * P, 3 * P)], start=True, stop=True)
            last = te.matmul(m.bank(2)[:, h * CTX:(h + 1) * CTX], q,
                             m.ht[0:DH, (h + 1) * self.KCOLS - CTX:(h + 1) * self.KCOLS], start=True, stop=True)
        last.then_inc(self.scored, 1)

    def p_v(self, pe, t, j):
        m, te = self.m, self.nc.tensor
        i = 4 * t + j
        pe.wait_ge(self.pt_sb, i + 1)
        pe.wait_ge(self.o_sb, i)
        for h in range(2):
            for c in range(5):
                tile = t + c if c < 3 else LT + 2 + c - 3
                last = te.matmul(m.bank(7)[:, h * DH:(h + 1) * DH],
                                 self.pt(j % 2)[:, (5 * h + c) * P:(5 * h + c + 1) * P],
                                 m.ht[:, ds(self.V_AT + tile * KVW + h * DH, DH)], start=(c == 0), stop=(c == 4))
        last.then_inc(self.product, 1)

    def transpose_o(self, pe, t, tp):
        m, te = self.m, self.nc.tensor
        pe.wait_ge(self.o_sb, 4 * t + 4)
        for k in range(4):
            last = te.transpose(m.bank(6)[:, k * P:(k + 1) * P], self.orow(tp)[:, k * P:(k + 1) * P], m.ident[:, :])
        last.then_inc(self.o_t, 1)

    def pe(self, pe):
        m, te = self.m, self.nc.tensor
        for t in range(NT):
            for h in range(KVH):
                last = te.transpose(m.ps[0:DH, (h * NT + t) * P:(h * NT + t + 1) * P],
                                    m.kv[:, t * 2 * KVW + h * DH:t * 2 * KVW + (h + 1) * DH], m.ident[:, :])
        last.then_inc(self.kt_made, 1)
        for half in range(2):
            if half:
                pe.wait_ge(self.q_sb, 1)
            self.transpose_q(pe, 0, 0, half)
        pe.wait_ge(self.keys_sb, 1)
        pe.wait_ge(self.padded, 1)
        pe.wait_ge(self.q_sb, 2)
        self.scores(pe, 0, 0, 0)

        def body(t, tp, least):
            for j in range(4):
                i = 4 * t + j
                if j:
                    self.p_v(pe, t, j - 1)
                elif least:
                    self.p_v(pe, t - 1, 3)
                pe.wait_ge(self.unloaded, i + 1)
                if j < 3:
                    self.scores(pe, t, tp, j + 1)
                elif least < LT - 1:
                    pe.wait_ge(self.q_sb, 2 * t + 4)
                    self.scores(pe, t + 1, 1 - tp, 0)
                pe.wait_ge(self.exped, i + 1)
                if least or j:
                    pe.wait_ge(self.pt_sb, i)
                for h in range(2):
                    for c in range(5):
                        last = te.transpose(m.ps[:, 3 * BANK + (5 * h + c) * P:3 * BANK + (5 * h + c + 1) * P],
                                            self.s_buf(j % 2)[:, h, c * P:(c + 1) * P], m.ident[:, :])
                last.then_inc(self.turned, 1)
                if j == 0 and least < LT - 1:
                    self.transpose_q(pe, t + 1, 1 - tp, 0)
                if j == 1 and least:
                    if least < LT - 1:
                        pe.wait_ge(self.q_sb, 2 * t + 3)
                    self.transpose_o(pe, t - 1, 1 - tp)
                if j == 2 and least < LT - 1:
                    if least:
                        pe.wait_ge(self.o_out, t)
                    else:
                        pe.wait_ge(self.q_sb, 3)
                    self.transpose_q(pe, t + 1, 1 - tp, 1)

        self.tiles(pe, body)
        self.p_v(pe, LT - 1, 3)
        pe.wait_ge(self.o_out, LT - 1)
        self.transpose_o(pe, LT - 1, (LT - 1) % 2)

    def act(self, act):
        m, a = self.m, self.nc.scalar

        def q_out(t, tp, half):
            act.wait_ge(self.q_t, 2 * t + half + 1)
            a.copy(self.q_t_buf(tp)[:, half * BANK:(half + 1) * BANK], m.bank(6)[0:DH, :]).then_inc(self.q_sb, 1)

        q_out(0, 0, 0)
        q_out(0, 0, 1)

        def pt_out(t, j, least):
            i = 4 * t + j
            act.wait_ge(self.turned, i + 1)
            if least or j >= 2:
                act.wait_ge(self.product, i - 1)
            a.copy(self.pt(j % 2), m.ps[:, 3 * BANK:3 * BANK + 2 * KEYS]).then_inc(self.pt_sb, 1)

        def o_out(t):
            act.wait_ge(self.o_t, t + 1)
            a.copy(m.mx[:, 0:4 * TOK].rearrange("p (k n) -> p k n", k=4)[:, :, ds(t * P, P)],
                   m.bank(6).rearrange("p (k n) -> p k n", k=4)).then_inc(self.o_out, 1)

        def body(t, tp, least):
            for j in range(4):
                i = 4 * t + j
                act.wait_ge(self.maxed, i + 1)
                for h in range(2):
                    s = self.s_buf(j % 2)[:, h, :]
                    a.activation(s, s, ACT.Exp, bias=self.small(j % 2, 1)[:, h:h + 1],
                                 accum_out=self.small(j % 2, 3)[:, h:h + 1])
                a.activation(self.small(j % 2, 2), self.small(j % 2, 2), ACT.Exp).then_inc(self.exped, 1)
                pt_out(t, j, least)
                if j == 1 and least:
                    o_out(t - 1)
                if j in (0, 2) and least < LT - 1:
                    q_out(t + 1, 1 - tp, j // 2)

        self.tiles(act, body)
        o_out(LT - 1)

    def dve(self, dve):
        m, v = self.m, self.nc.vector
        dve.wait_ge(self.kt_made, 1)
        for h in range(KVH):
            src = m.ps[0:DH, h * NT * P:(h + 1) * NT * P]
            v.tensor_copy(self.key_columns(h)[:, P:(LT + 1) * P], src[:, 0:LT * P])
            last = v.tensor_copy(self.key_columns(h)[:, (LT + 2) * P:], src[:, LT * P:])
        last.then_inc(self.keys_sb, 1)
        dve.wait_ge(self.sink, 16)
        v.tensor_scalar(self.negated_sink(), self.negated_sink(), -1.0, None, ALU.mult)
        dve.wait_ge(self.padded, 1)
        masks = m.w[:, self.MASK_AT:self.SMALL_AT].rearrange("p (i c) -> p i c", i=3)

        def normed(t, j, tp):
            s = j % 2
            i = 4 * t + j
            dve.wait_ge(self.exped, i + 1)
            v.tensor_tensor(self.small(s, 4), self.small(s, 3), self.small(s, 2), ALU.add)
            dve.drain()
            v.reciprocal(self.small(s, 4), self.small(s, 4))
            dve.drain()
            dve.wait_ge(self.product, i + 1)
            out = self.orow(tp).rearrange("p (h j d) -> p j h d", h=2, j=4)[:, j]
            v.tensor_tensor(out, m.bank(7, 2 * DH).rearrange("p (h d) -> p h d", h=2),
                            along(self.small(s, 4), 2, [P, 2, DH]), ALU.mult).then_inc(self.o_sb, 1)

        def body(t, tp, least):
            mask = 0 if least == 0 else 2 if least == LT - 1 else 1
            for j in range(4):
                i, s = 4 * t + j, j % 2
                buf = self.s_buf(s)
                dve.wait_ge(self.scored, i + 1)
                if least or j >= 2:
                    dve.wait_ge(self.turned, i - 1)
                v.scalar_tensor_tensor(buf[:, :, 0:3 * P], m.ps[:, 0:2 * BANK].rearrange("p (h c) -> p h c", h=2)[:, :, 0:3 * P],
                                       DH ** -0.5, along(masks[:, mask, :], 1, [P, 2, 3 * P]), ALU.mult, ALU.add)
                v.tensor_scalar(buf[:, :, 3 * P:], m.bank(2).rearrange("p (h c) -> p h c", h=2), DH ** -0.5, None,
                                ALU.mult).then_inc(self.unloaded, 1)
                dve.drain()
                v.tensor_reduce(self.small(s, 0), buf, AX.X, ALU.max)
                dve.drain()
                sink = self.negated_sink().rearrange("p (h j) -> p j h", h=2)[:, j]
                v.scalar_tensor_tensor(self.small(s, 1), self.small(s, 0), -1.0, sink, ALU.mult, ALU.min)
                dve.drain()
                v.tensor_tensor(self.small(s, 2), self.small(s, 1), sink, ALU.subtract).then_inc(self.maxed, 1)
                if j:
                    normed(t, j - 1, tp)
                elif least:
                    normed(t - 1, 3, 1 - tp)

        self.tiles(dve, body)
        normed(LT - 1, 3, (LT - 1) % 2)


class Route(Stage):

    BIAS, MX8, IX8, IXF, GK, GS, DK, CNT, PAD, PEND, PSTART, EB, ENT = (
        0, 64, 144, 224, 284, 344, 354, 414, 478, 542, 606, 670, 680)
    ONES = 800
    JUNK = 864
    SIG, SEL, OH, PR, MASKF, MASKB = 0, 640, 1280, 5120, 8960, 9600
    SCATTER_FROM = 4

    def __init__(self, m, layer, tiles, experts):
        super().__init__(m)
        self.shared_w, self.bias, self.gate_up, self.silu_done, self.h_made = self.signals("route", "shared_w bias gate_up silu_done h_made")
        self.h_t, self.ht_sb, self.down, self.y_sb, self.sig = self.signals("route", "h_t ht_sb down y_sb sig")
        self.mask, self.ranked, self.default_made, self.default_stored, self.placed = self.signals("route", "mask ranked default_made default_stored placed")
        self.table, self.expert_out, self.regs_in = self.signals("route", "table expert_out regs_in")
        self.ys = [self.own(f"route_y{i}") for i in range(2)]
        self.scattered = m.sem(f"route_scattered_{layer}")
        self.layer, self.n, self.experts = layer, tiles, experts

    def gt(self, at, n):
        return self.m.gt[:, at:at + n]

    def sync(self, sp):
        m, io, L, n = self.m, self.m.io, self.layer, self.n
        for part in expert_parts(m, 2 * SLOT, io["sh_w_gate"][L], io["sh_w_up"][L], io["sh_w_down"][L]):
            sp.dma_start(*part).then_inc(self.shared_w, 16)
        sp.dma_start(self.gt(self.BIAS, NE), bcast(io["router_b"][L])).then_inc(self.bias, 16)
        for s in self.experts.wl:
            sp.sem_inc(s)
        for e in range(2):
            self.experts.load(sp, e, e)
        sp.wait_ge(self.default_made, 2)
        sp.dma_start(m.slot_table.rearrange("(p b) c -> p (b c)", b=TABLE),
                     m.slots[:, :, :].rearrange("p b c -> p (b c)")).then_inc(self.default_stored, 16)
        for t in range(n):
            sp.wait_ge(self.y_sb, t + 1)
            sp.dma_start(m.y[t * P:(t + 1) * P, :], m.bc[:, (t % 2) * D:(t % 2 + 1) * D]).then_inc(self.ys[t % 2], 16)
            if t == self.SCATTER_FROM - 1:
                sp.wait_ge(self.placed, 1)
                sp.dma_start(m.block_expert, self.gt(self.EB, 1).bitcast(I32)).then_inc(self.expert_out, 16)
                sp.wait_ge(self.expert_out, 16)
                sp.dma_start(m.regs[0:1, 0:P], m.block_expert.rearrange("b o -> o b")).then_inc(self.regs_in, 16)
        for i in range(2):
            sp.wait_ge(self.ys[i], 8 * n)
        sp.wait_ge(self.scattered, 16 * n * TOPK)
        sp.dma_start(m.slots[:, :, :], m.slot_table.rearrange("(b p) c -> p b c", p=P)).then_inc(self.table, 16)
        sp.wait_ge(self.table, 16)
        sp.wait_ge(self.regs_in, 16)

    def pool(self, pool):
        m, g, n = self.m, self.nc.gpsimd, self.n
        g.iota(m.slots[:, :, 0], [[1, TABLE]], base=0, channel_multiplier=TABLE)
        ent = self.gt(self.ENT, n * TOPK * 2).bitcast(I32).rearrange("p (i c) -> p i c", c=2)
        g.iota(ent[:, :, 0].rearrange("p (t k) -> p t k", k=TOPK), [[P, n], [0, TOPK]], base=0, channel_multiplier=1)
        g.memset(self.gt(self.ONES, NE), 1.0).then_inc(self.default_made, 1)
        start, done = self.SCATTER_FROM, 0
        for t in range(n):
            pool.wait_ge(self.silu_done, 2 * t + 2)
            if t:
                pool.wait_ge(self.h_t, t)
            g.tensor_tensor(m.st[:, D + 512:D + 768], m.st[:, D:D + 256], m.st[:, D + 256:D + 512],
                            ALU.mult).then_inc(self.h_made, 1)
            if t < start:
                continue
            if t == start:
                pool.wait_ge(self.placed, 1)
                pool.wait_ge(self.default_stored, 16)
            upto = n * TOPK * (t - start + 1) // (n - start)
            for i in range(done, upto):
                g.indirect_dma_start(out=m.slot_table, out_offset=bass.IndirectOffsetOnAxis(
                    ap=self.gt(self.DK + i, 1).bitcast(I32), axis=0), in_=ent[:, i, :], in_offset=None).then_inc(self.scattered, 16)
            done = upto

    def h_tile(self, t):
        return lambda k: self.m.ht[:, k * TOK + t * P:k * TOK + (t + 1) * P]

    def pe(self, pe):
        m, te, n = self.m, self.nc.tensor, self.n
        w = self.m.w[:, 2 * SLOT:3 * SLOT]
        pe.wait_ge(self.shared_w, 48)

        def finish(t):
            pe.wait_ge(self.h_made, t + 1)
            for k in range(2):
                last = te.transpose(m.bank(2)[:, k * P:(k + 1) * P], h_slab(m.st[:, D + 512:D + 768], k), m.ident[:, :])
            last.then_inc(self.h_t, 1)
            pe.wait_ge(self.ht_sb, t + 1)
            if t:
                pe.wait_ge(self.y_sb, t)
            down_product(te, m, m.st[:, D + 768:D + 1024], w[:, 2 * KT * DE:], 3).then_inc(self.down, 1)

        for t in range(n):
            if t >= 2:
                pe.wait_ge(self.silu_done, 2 * t - 2)
            gate_up_product(te, m.bank(t % 2), self.h_tile(t), w[:, 0:2 * KT * DE]).then_inc(self.gate_up, 1)
            if t:
                finish(t - 1)
            if t == 2:
                self.ranks(pe)
        finish(n - 1)

    def ranks(self, pe):
        m, te, n = self.m, self.nc.tensor, self.n
        mask = m.mx[:, self.MASKB:self.MASKB + n * NE // 2].bitcast(BF16)
        pe.wait_ge(self.mask, 1)
        for t in range(n + 1):
            out = m.ps[:, 6 * BANK + t * NE:6 * BANK + (t + 1) * NE]
            for u in range(min(t + 1, n)):
                last = te.matmul(out, m.before[:, :] if u == t else m.ones[:, :], mask[:, u * NE:(u + 1) * NE],
                                 start=(u == 0), stop=(u == min(t, n - 1)))
        last.then_inc(self.ranked, 1)

    def act(self, act):
        m, a, n = self.m, self.nc.scalar, self.n
        a.activation(m.mx[:, self.SIG:self.SIG + n * NE], m.logits[:, 0:n, :].rearrange("p t e -> p (t e)"),
                     ACT.Sigmoid).then_inc(self.sig, 1)

        def finish(t):
            act.wait_ge(self.h_t, t + 1)
            if t:
                act.wait_ge(self.down, t)
            a.copy(m.st[:, D + 768:D + 1024], m.bank(2, 256)).then_inc(self.ht_sb, 1)
            act.wait_ge(self.down, t + 1)
            if t >= 2:
                act.wait_ge(self.ys[t % 2], 16 * (t // 2))
            a.copy(m.bc[:, (t % 2) * D:(t % 2 + 1) * D], m.ps[:, 3 * BANK:5 * BANK]).then_inc(self.y_sb, 1)

        for t in range(n):
            act.wait_ge(self.gate_up, t + 1)
            if t:
                act.wait_ge(self.h_made, t)
            a.activation(m.st[:, D:D + 256], m.bank(t % 2)[:, 0:256], ACT.Silu).then_inc(self.silu_done, 1)
            a.copy(m.st[:, D + 256:D + 512], m.bank(t % 2)[:, 256:512]).then_inc(self.silu_done, 1)
            if t:
                finish(t - 1)
        finish(n - 1)

    def dve(self, dve):
        m, v, n = self.m, self.nc.vector, self.n
        N = n * TOPK
        mx = lambda at, k: m.mx[:, at:at + k]
        dve.wait_ge(self.default_made, 1)
        v.tensor_scalar(m.slots[:, :, 0], m.slots[:, :, 0], P - 1, DUMMY, ALU.bitwise_and, ALU.bitwise_or)
        v.memset(m.slots[:, :, 1], 0).then_inc(self.default_made, 1)
        dve.wait_ge(self.sig, 1)
        dve.wait_ge(self.bias, 16)
        v.tensor_tensor(mx(self.SEL, n * NE).rearrange("p (t e) -> p t e", e=NE),
                        mx(self.SIG, n * NE).rearrange("p (t e) -> p t e", e=NE),
                        along(self.gt(self.BIAS, NE), 1, [P, n, NE]), ALU.add)
        dve.drain()
        for t in range(n):
            v.max(self.gt(self.MX8 + 8 * t, 8), mx(self.SEL + t * NE, NE))
        dve.drain()
        for t in range(n):
            v.max_index(self.gt(self.IX8 + 8 * t, 8).bitcast(U32), self.gt(self.MX8 + 8 * t, 8), mx(self.SEL + t * NE, NE))
        dve.drain()
        v.tensor_copy(self.gt(self.IXF, N).rearrange("p (t k) -> p t k", k=TOPK),
                      self.gt(self.IX8, 8 * n).bitcast(U32).rearrange("p (t k) -> p t k", k=8)[:, :, 0:TOPK])
        dve.drain()
        onehot = mx(self.OH, N * NE).rearrange("p (i e) -> p i e", e=NE)
        product = mx(self.PR, N * NE).rearrange("p (i e) -> p i e", e=NE)
        v.tensor_tensor(onehot, along(m.iota_e[:, :], 1, [P, N, NE]), along(self.gt(self.IXF, N), 2, [P, N, NE]), ALU.is_equal)
        dve.drain()
        maskf = mx(self.MASKF, n * NE)
        v.tensor_reduce(maskf.rearrange("p (t e) -> p t e", e=NE),
                        mx(self.OH, N * NE).rearrange("p (t k e) -> p t e k", k=TOPK, e=NE), AX.X, ALU.add)
        dve.drain()
        v.tensor_copy(mx(self.MASKB, n * NE // 2).bitcast(BF16), maskf).then_inc(self.mask, 1)

        def picked(table, at):
            v.tensor_tensor(product.rearrange("p (t k) e -> p t k e", k=TOPK), onehot.rearrange("p (t k) e -> p t k e", k=TOPK),
                            table.rearrange("p (t e) -> p t e", e=NE).unsqueeze(2).broadcast_to([P, n, TOPK, NE]), ALU.mult)
            dve.drain()
            v.tensor_reduce(self.gt(at, N), product, AX.X, ALU.add)
            dve.drain()

        picked(mx(self.SIG, n * NE), self.GK)
        gk = self.gt(self.GK, N).rearrange("p (t k) -> p t k", k=TOPK)
        v.tensor_reduce(self.gt(self.GS, n), gk, AX.X, ALU.add)
        dve.drain()
        v.tensor_scalar(self.gt(self.GS, n), self.gt(self.GS, n), 1e-20, None, ALU.add)
        dve.drain()
        v.reciprocal(self.gt(self.GS, n), self.gt(self.GS, n))
        dve.drain()
        v.tensor_tensor(gk, gk, along(self.gt(self.GS, n), 2, [P, n, TOPK]), ALU.mult)
        dve.drain()
        ent = self.gt(self.ENT, N * 2).rearrange("p (i c) -> p i c", c=2)
        v.tensor_scalar(ent[:, :, 1], self.gt(self.GK, N), SCALE_ROUTED, None, ALU.mult)
        dve.wait_ge(self.ranked, 1)
        counts = m.ps[:, 6 * BANK + n * NE:6 * BANK + (n + 1) * NE]
        cnt = self.gt(self.CNT, NE).bitcast(I32)
        pad, pend, pstart = self.gt(self.PAD, NE), self.gt(self.PEND, NE), self.gt(self.PSTART, NE)
        v.tensor_scalar(cnt, counts, float(P - 1), None, ALU.add)
        dve.drain()
        v.tensor_scalar(cnt, cnt, 7, 7, ALU.logical_shift_right, ALU.logical_shift_left)
        dve.drain()
        v.tensor_copy(pad, cnt)
        dve.drain()
        v.tensor_tensor_scan(pend, self.gt(self.ONES, NE), pad, 0.0, ALU.mult, ALU.add)
        dve.drain()
        v.tensor_tensor(pstart, pend, pad, ALU.subtract)
        v.tensor_scalar(self.gt(self.JUNK, NE), pend, m.iota_blk[:, :], None, ALU.is_le, ALU.add, accum_out=self.gt(self.EB, 1))
        v.tensor_scalar(m.regs[0:1, 2 * P:2 * P + 1], pend[0:1, NE - 1:NE], 1.0 / P, None, ALU.mult)
        dve.drain()
        v.tensor_scalar(m.regs[0:1, P:P + NE], pstart[0:1, :], 1.0 / P, None, ALU.mult)
        v.tensor_scalar(self.gt(self.JUNK, 1), self.gt(self.EB, 1), float(NE - 1), None, ALU.min)
        v.tensor_tensor(mx(self.SEL, n * NE).rearrange("p (t e) -> p t e", e=NE),
                        m.ps[:, 6 * BANK:6 * BANK + n * NE].rearrange("p (t e) -> p t e", e=NE),
                        along(pstart, 1, [P, n, NE]), ALU.add)
        dve.drain()
        v.tensor_copy(self.gt(self.EB, 1).bitcast(I32), self.gt(self.JUNK, 1))
        picked(mx(self.SEL, n * NE), self.GK)
        v.tensor_copy(self.gt(self.DK, N).bitcast(I32), self.gt(self.GK, N)).then_inc(self.placed, 1)


def expert_parts(m, at, gate, up, down):
    n = KT * DE
    cut = lambda o, k: m.w[:, ds(at + o, n)].rearrange("p (k n) -> p k n", k=k)
    return [(cut(0, KT), gate.rearrange("(p k) n -> p k n", k=KT)),
            (cut(n, KT), up.rearrange("(p k) n -> p k n", k=KT)),
            (cut(2 * n, 2), down.rearrange("(p k) n -> p k n", k=2))]


def gate_up_product(te, bank, tile, w):
    both = w.rearrange("p (h k n) -> p k h n", h=2, k=KT)
    for k in range(KT):
        last = te.matmul(bank.rearrange("p (h n) -> p h n", h=2), tile(k), both[:, k], start=(k == 0), stop=(k == KT - 1))
    return last


def h_slab(h, k):
    return h.rearrange("p (c k) -> p k c", k=2)[:, k, :]


def down_product(te, m, h_t, w, bank):
    down = w.rearrange("p (k n) -> p k n", k=2)
    for half in range(2):
        for k in range(2):
            last = te.matmul(m.bank(bank + half), h_t[:, k * P:(k + 1) * P], down[:, k, half * BANK:(half + 1) * BANK],
                             start=(k == 0), stop=(k == 1))
    return last


class Experts(Stage):

    def __init__(self, m, layer, tiles):
        super().__init__(m)
        self.index, self.x_t, self.xt_a, self.xt_d, self.gate_up = self.signals("moe", "index x_t xt_a xt_d gate_up")
        self.silu_done, self.h_made, self.h_t, self.ht_sb, self.down = self.signals("moe", "silu_done h_made h_t ht_sb down")
        self.y_a, self.y_d, self.pool_settled = self.signals("moe", "y_a y_d pool_settled")
        self.layer, self.nblk = layer, blocks_bound(tiles * P)
        self.wl = [self.own(f"moe_w{i}") for i in range(2)]
        self.xl = [m.sem(f"moe_rows{i}_{layer}") for i in range(2)]
        self.added = m.sem(f"moe_added_{layer}")

    def load(self, sp, e, parity):
        io, L = self.m.io, self.layer
        for dst, src in expert_parts(self.m, parity * SLOT, *(
                io[f"exp_w_{s}"][L, ds(e, 1)].rearrange("o r n -> (o r) n") for s in ("gate", "up", "down"))):
            sp.dma_start(dst, src).then_inc(self.wl[parity], 16)

    def used(self, eng):
        return eng.value_load(self.m.regs[0:1, 2 * P:2 * P + 1], min_val=1, max_val=self.nblk)

    def blocks(self, eng, body):
        used = self.used(eng)
        body(0, 0)
        with eng.Fori(0, self.nblk // 2) as i:
            for half in range(2):
                b = 2 * i + (1 + half)
                with eng.If(b < used):
                    body(b, 1 - half)

    def sync(self, sp):
        m = self.m
        with sp.Fori(1, NE // 2) as i:
            for parity in range(2):
                e = 2 * i + parity
                first = sp.value_load(m.regs[0:1, ds(P + e - 1, 1)], min_val=0, max_val=self.nblk)
                sp.wait_ge(self.down, first + 1)
                self.load(sp, e, parity)
        for parity in range(2):
            sp.wait_ge(self.wl[parity], 48 * NE // 2 + 1)

    def rows(self, parity):
        return self.m.bc[:, parity * D:(parity + 1) * D]

    def rows_t(self, parity):
        return self.m.bc[:, (2 + parity) * D:(3 + parity) * D]

    def pool(self, pool):
        m, g = self.m, self.nc.gpsimd

        def take_index(b, i, taken):
            g.tensor_copy(m.index[:, i:i + 1],
                          m.slots[:, ds(b, 1), 0:1].rearrange("p b c -> p (b c)")).then_inc(self.index, 1)
            pool.wait_ge(self.index, taken)
            settle(pool, self.pool_settled)

        def fetch(b, parity, taken):
            take_index(b, parity, taken)
            g.indirect_dma_start(out=self.rows(parity), out_offset=None, in_=m.h2, in_offset=bass.IndirectOffsetOnAxis(
                ap=m.index[:, parity:parity + 1], axis=0)).then_inc(self.xl[parity], 16)

        fetch(0, 0, 1)
        fetch(1, 1, 2)

        def body(b, parity):
            pool.wait_ge(self.x_t, b + 1)
            fetch(b + 2, parity, 2 * b + 3)
            take_index(b, 2 + parity, 2 * b + 4)
            pool.wait_ge(self.y_a, b + 1)
            pool.wait_ge(self.y_d, b + 1)
            wait_some(pool, self.added, 16 * b)
            settle(pool, self.pool_settled)
            g.indirect_dma_start(out=m.y, out_offset=bass.IndirectOffsetOnAxis(ap=m.index[:, 2 + parity:3 + parity], axis=0),
                                 in_=m.st[:, 0:D], in_offset=None, compute_op=ALU.add).then_inc(self.added, 16)

        self.blocks(pool, body)
        pool.wait_ge(self.added, 16 * self.used(pool))
        for parity in range(2):
            pool.wait_ge(self.xl[parity], 16)
        settle(pool, self.pool_settled)

    def transpose_block(self, pe, b, parity):
        m = self.m
        pe.wait_ge(self.xl[parity], 8 * (b - parity) + 16)
        wait_some(pe, self.xt_a, b)
        wait_some(pe, self.xt_d, b)
        transpose_rows(self.nc.tensor, m, self.rows(parity), 1).then_inc(self.x_t, 1)

    def pe(self, pe):
        m, te = self.m, self.nc.tensor
        self.transpose_block(pe, 0, 0)
        pe.sem_inc(self.down)

        def body(b, parity):
            e = pe.value_load(m.regs[0:1, ds(b, 1)], min_val=0, max_val=NE - 1)
            pe.wait_ge(self.wl[0], (e // 2) * 48 + 49)
            pe.wait_ge(self.wl[1], ((e + 1) // 2) * 48 + 1)
            pe.wait_ge(self.xt_a, b + 1)
            pe.wait_ge(self.xt_d, b + 1)
            w = (e % 2) * SLOT
            gate_up_product(te, m.bank(0), lambda k: self.rows_t(parity)[:, k * P:(k + 1) * P],
                            m.w[:, ds(w, 2 * KT * DE)]).then_inc(self.gate_up, 1)
            self.transpose_block(pe, b + 1, 1 - parity)
            pe.wait_ge(self.h_made, b + 1)
            for k in range(2):
                last = te.transpose(m.bank(3)[:, k * P:(k + 1) * P], h_slab(m.st[:, D + 256:D + 512], k), m.ident[:, :])
            last.then_inc(self.h_t, 1)
            pe.wait_ge(self.ht_sb, b + 1)
            wait_some(pe, self.y_a, b)
            wait_some(pe, self.y_d, b)
            down_product(te, m, m.st[:, D + 512:D + 768], m.w[:, ds(w + 2 * KT * DE, 2 * D)], 4).then_inc(self.down, 1)

        self.blocks(pe, body)

    def gate(self, b):
        return self.m.slots[:, ds(b, 1), 1:2].rearrange("p b c -> p (b c)").bitcast(F32)

    def act(self, act):
        m, a = self.m, self.nc.scalar

        def half_a(b, parity):
            act.wait_ge(self.x_t, b + 1)
            a.copy(self.rows_t(parity)[:, 0:512], m.bank(1)).then_inc(self.xt_a, 1)

        half_a(0, 0)

        def body(b, parity):
            act.wait_ge(self.gate_up, b + 1)
            wait_some(act, self.h_made, b)
            a.activation(m.st[:, D:D + 256], m.bank(0)[:, 0:256], ACT.Silu).then_inc(self.silu_done, 1)
            half_a(b + 1, 1 - parity)
            act.wait_ge(self.h_t, b + 1)
            act.wait_ge(self.down, b + 1)
            a.copy(m.st[:, D + 512:D + 768], m.bank(3, 256)).then_inc(self.ht_sb, 1)
            act.wait_ge(self.down, b + 2)
            wait_some(act, self.added, 16 * b)
            a.activation(m.st[:, 0:512], m.bank(4), ACT.Copy, scale=self.gate(b)).then_inc(self.y_a, 1)

        self.blocks(act, body)

    def dve(self, dve):
        m, v = self.m, self.nc.vector

        def half_d(b, parity):
            dve.wait_ge(self.x_t, b + 1)
            v.tensor_copy(self.rows_t(parity)[:, 512:1024], m.bank(2)).then_inc(self.xt_d, 1)

        half_d(0, 0)

        def body(b, parity):
            dve.wait_ge(self.silu_done, b + 1)
            wait_some(dve, self.h_t, b)
            v.tensor_tensor(m.st[:, D + 256:D + 512], m.st[:, D:D + 256], m.bank(0)[:, 256:512], ALU.mult).then_inc(self.h_made, 1)
            half_d(b + 1, 1 - parity)
            dve.wait_ge(self.down, b + 2)
            wait_some(dve, self.added, 16 * b)
            v.tensor_scalar(m.st[:, 512:1024], m.bank(5), self.gate(b), None, ALU.mult).then_inc(self.y_d, 1)

        self.blocks(dve, body)


class Output(Stage):

    def __init__(self, m):
        super().__init__(m)
        self.gate, self.gated, self.ready = self.signals("final", "gate gated ready")
        self.xl = [self.own(f"final_x{i}") for i in range(2)]
        self.xs = [self.own(f"final_s{i}") for i in range(2)]

    def x(self, t):
        return self.m.bc[:, (t % 2) * D:(t % 2 + 1) * D]

    def y(self, t):
        return self.m.bc[:, (2 + t % 2) * D:(3 + t % 2) * D]

    def sync(self, sp):
        m, out = self.m, self.m.io["out"]
        sp.dma_start(m.gt[:, 0:D], bcast(m.modrow[1, 0, 5 * D:6 * D])).then_inc(self.gate, 16)
        for t in range(LT + 1):
            if t < LT:
                if t >= 2:
                    sp.wait_ge(self.xs[t % 2], 16 * (t // 2))
                    sp.wait_ge(self.ready, t - 1)
                sp.dma_start(self.x(t), m.xres[t * P:(t + 1) * P, :]).then_inc(self.xl[t % 2], 16)
                sp.dma_start(self.y(t), m.y[t * P:(t + 1) * P, :]).then_inc(self.xl[t % 2], 16)
            if t:
                u = t - 1
                sp.wait_ge(self.ready, u + 1)
                sp.dma_start(out[0, u * P:(u + 1) * P, :], self.x(u)).then_inc(self.xs[u % 2], 16)
        for i in range(2):
            sp.wait_ge(self.xs[i], 16 * LT // 2)

    def dve(self, dve):
        m, v = self.m, self.nc.vector
        dve.wait_ge(self.gate, 16)
        for t in range(LT):
            dve.wait_ge(self.xl[t % 2], 32 * (t // 2 + 1))
            v.tensor_tensor(self.y(t), self.y(t), m.gt[:, 0:D], ALU.mult)
            dve.drain()
            v.tensor_tensor(self.x(t), self.x(t), self.y(t), ALU.add).then_inc(self.ready, 1)


def build(nc, io, upto=99):
    with ExitStack() as ctx:
        m = Machine(nc, ctx, io)
        experts = [Experts(m, 0, NT), Experts(m, 1, LT)]
        stages = [Setup(m), Modulation(m, 0), NormIn(m, 0), EvenProjections(m), Fourier(m), MixOut(m, 0, NT),
                  Route(m, 0, NT, experts[0]), experts[0],
                  Modulation(m, 1), NormIn(m, 1), OddProjections(m), Attention(m), MixOut(m, 1, LT),
                  Route(m, 1, LT, experts[1]), experts[1], Output(m)][:upto]
        block = ctx.enter_context(nc.Block())

        @block.sync
        def _(sp):
            for n, stage in enumerate(stages):
                stage.sync(sp)
                m.meet(sp, 2 * n + 1)
                for s in stage.mine:
                    sp.sem_clear(s)
                m.meet(sp, 2 * n + 2)

        @block.gpsimd
        def _(pool):
            for n, stage in enumerate(stages):
                stage.pool(pool)
                m.meet(pool, 2 * n + 1)
                m.meet(pool, 2 * n + 2)

        @block.scalar
        def _(act):
            for n, stage in enumerate(stages):
                stage.act(act)
                m.meet(act, 2 * n + 1)
                m.meet(act, 2 * n + 2)

        @block.vector
        def _(dve):
            for n, stage in enumerate(stages):
                stage.dve(dve)
                m.meet(dve, 2 * n + 1)
                m.meet(dve, 2 * n + 2)

        @block.tensor
        def _(pe):
            for n, stage in enumerate(stages):
                stage.pe(pe)
                m.meet(pe, 2 * n + 1)
                m.meet(pe, 2 * n + 2)


def shape_tables():
    def dft(rows, cols, size):
        angle = 2 * np.pi * (np.outer(rows, cols) % size) / size
        return np.cos(angle), np.sin(angle)

    n = P
    c, s = dft(np.arange(n), np.arange(n), n)
    channel = np.concatenate([c, s], 1)
    scale = 1 / np.sqrt(SEQ * n)
    c, s = dft(np.arange(SEQ), np.arange(SEQ // 2), SEQ)
    seq = (np.stack([c, s], 1) * scale).reshape(LT, P, 2 * SEQ // 2).transpose(1, 0, 2).reshape(P, -1)
    mid = (np.cos(np.pi * np.arange(SEQ)) * scale).reshape(LT, P).T
    c, s = dft(np.arange(CTX), np.arange(CTX), CTX)
    small = (np.stack([c, -s], 1) / np.sqrt(CTX * n)).reshape(CT, P, 2 * CTX).transpose(1, 0, 2).reshape(P, -1)
    grid = 64
    pos = np.arange(SEQ)
    inv = np.float32(10000.0) ** (-np.arange(0, DH // 2, 2, dtype=np.float32) / np.float32(DH // 2))
    angle = np.stack([(pos // grid).astype(np.float32)[:, None] * inv, (pos % grid).astype(np.float32)[:, None] * inv], 1)
    lay = lambda x: x.reshape(LT, P, 2 * ROPE).transpose(1, 0, 2).reshape(P, -1)
    rope = np.concatenate([lay(np.cos(angle)), lay(np.sin(angle))], 1)
    return {k: np.ascontiguousarray(v, dtype=np.float32) for k, v in (
        ("dft_channel", channel), ("dft_seq", seq), ("dft_mid", mid), ("dft_ctx", small), ("rope", rope))}


INPUTS = ["x", "c", "ctx", "c_ctx", "ada_w", "ada_b", "norm1_g", "norm2_g", "ev_w_in", "ev_w_s", "ev_b_s", "ev_w_out",
          "od_w_in", "od_q_norm_g", "od_k_norm_g", "od_sink", "od_conv_w", "od_w_out", "router_w", "router_b",
          "exp_w_gate", "exp_w_up", "exp_w_down", "sh_w_gate", "sh_w_up", "sh_w_down"]


def kernel(**inputs):
    import concourse.bacc as bacc
    from concourse.bass_utils import run_bass_kernel_spmd

    nc = bacc.Bacc("TRN2", target_bir_lowering=False, num_devices=1)
    arrays = {name: np.ascontiguousarray(inputs[name]) for name in INPUTS}
    arrays.update(shape_tables())
    io = {name: nc.dram_tensor(name, a.shape, mybir.dt.from_np(a.dtype), kind="ExternalInput").ap()
          for name, a in arrays.items()}
    io["out"] = nc.dram_tensor("out", (1, SEQ, D), F32, kind="ExternalOutput").ap()
    build(nc, io)
    return run_bass_kernel_spmd(nc, [arrays], core_ids=[0]).results[0]["out"]
```
